# Optimizing a Trainium2 kernel written in Bass

```python
import math
import jax, jax.numpy as jnp
from jax import lax
import numpy as np

D_MODEL = 1024
BATCH = 1
SEQ = 1024
DEPTH = 1

CHUNK = 64
WINDOW = 128
WIN_CHUNKS = WINDOW // CHUNK
HEAD_DIM = 64
N_Q_HEADS = 8
N_KV_HEADS = 2
GQA_GROUP = N_Q_HEADS // N_KV_HEADS
ATTN_WIDTH = N_Q_HEADS * HEAD_DIM
KV_WIDTH = N_KV_HEADS * HEAD_DIM
ROPE_THETA = 10000.0
SSM_WIDTH = D_MODEL // 2
SSM_GROUP = 16
SSM_GROUPS = SSM_WIDTH // SSM_GROUP
SSM_STATE = 64
DT_MIN = 0.001
DT_MAX = 0.1
MEM_LEN = 256
X_HEADS = 4
X_HEAD_DIM = 128
X_WIDTH = X_HEADS * X_HEAD_DIM
N_BRANCH = 3
D_FF = 4 * D_MODEL
EPS = 1e-6
NEG_INF = -1e30

_IN_SIZES = [ATTN_WIDTH, KV_WIDTH, KV_WIDTH, SSM_WIDTH, X_WIDTH, N_BRANCH * D_MODEL]
_IN_SPLITS = [int(v) for v in np.cumsum(_IN_SIZES)[:-1]]
IN_COLS = int(sum(_IN_SIZES))

kernel_name = 'chunk_causal_hybrid_swa_s5_memxattn_block'

def rmsnorm(x, g):
    xf = x.astype(jnp.float32)
    y = xf * lax.rsqrt(jnp.mean(xf * xf, axis=-1, keepdims=True) + EPS)
    return (y * g.astype(jnp.float32)).astype(x.dtype)

def rope(t, positions):
    half = t.shape[-1] // 2
    inv_freq = ROPE_THETA ** (-jnp.arange(half, dtype=jnp.float32) / half)
    ang = positions.astype(jnp.float32)[..., None] * inv_freq
    cos = jnp.cos(ang)[:, :, None, :]
    sin = jnp.sin(ang)[:, :, None, :]
    tf = t.astype(jnp.float32)
    t1, t2 = tf[..., :half], tf[..., half:]
    return jnp.concatenate([t1 * cos - t2 * sin, t2 * cos + t1 * sin], axis=-1).astype(t.dtype)

def _band_keys(t):
    parts = []
    for j in range(WIN_CHUNKS - 1, 0, -1):
        pad = [(0, 0), (j, 0)] + [(0, 0)] * (t.ndim - 2)
        parts.append(jnp.pad(t, pad)[:, :-j])
    parts.append(t)
    return jnp.concatenate(parts, axis=2)

def sliding_window_attention(q, k, v, sinks):
    B, L = q.shape[0], q.shape[1]
    nC = L // CHUNK
    W = WIN_CHUNKS * CHUNK
    qc = q.reshape(B, nC, CHUNK, N_KV_HEADS, GQA_GROUP, HEAD_DIM)
    kc = _band_keys(k.reshape(B, nC, CHUNK, N_KV_HEADS, HEAD_DIM))
    vc = _band_keys(v.reshape(B, nC, CHUNK, N_KV_HEADS, HEAD_DIM))
    s = jnp.einsum('bnqhgd,bnshd->bnhgqs', qc, kc,
                   preferred_element_type=jnp.float32) * (HEAD_DIM ** -0.5)
    chunk_idx = jnp.arange(nC)[:, None]
    back = (WIN_CHUNKS - 1) - jnp.arange(W)[None, :] // CHUNK
    valid = (chunk_idx - back >= 0).reshape(1, nC, 1, 1, 1, W)
    s = jnp.where(valid, s, NEG_INF)
    sink = sinks.astype(jnp.float32).reshape(1, 1, N_KV_HEADS, GQA_GROUP, 1, 1)
    m = jnp.maximum(jnp.max(s, axis=-1, keepdims=True), sink)
    p = jnp.exp(s - m)
    denom = jnp.sum(p, axis=-1, keepdims=True) + jnp.exp(sink - m)
    o = jnp.einsum('bnhgqs,bnshd->bnqhgd', (p / denom).astype(vc.dtype), vc)
    return o.reshape(B, L, ATTN_WIDTH)

def memory_cross_attention(qx, km, vm):
    B, L = qx.shape[0], qx.shape[1]
    q = qx.reshape(B, L, X_HEADS, X_HEAD_DIM)
    s = jnp.einsum('blhd,bmhd->bhlm', q, km,
                   preferred_element_type=jnp.float32) * (X_HEAD_DIM ** -0.5)
    p = jax.nn.softmax(s, axis=-1).astype(vm.dtype)
    o = jnp.einsum('bhlm,bmhd->blhd', p, vm)
    return o.reshape(B, L, X_WIDTH)

def _ssm_combine(e1, e2):
    a1r, a1i, b1r, b1i = e1
    a2r, a2i, b2r, b2i = e2
    return (a2r * a1r - a2i * a1i,
            a2r * a1i + a2i * a1r,
            a2r * b1r - a2i * b1i + b2r,
            a2r * b1i + a2i * b1r + b2i)

def s5_branch(u, A_re, A_im, log_dt, B_re, B_im, C_re, C_im, D_skip, w_glu):
    Bsz, L = u.shape[0], u.shape[1]
    f32 = jnp.float32
    uf = u.astype(f32).reshape(Bsz, L, SSM_GROUPS, SSM_GROUP)
    ar, ai = A_re.astype(f32), A_im.astype(f32)
    dt = jnp.exp(log_dt.astype(f32))[:, None]
    mag = jnp.exp(ar * dt)
    ab_re, ab_im = mag * jnp.cos(ai * dt), mag * jnp.sin(ai * dt)
    den = ar * ar + ai * ai
    n_re, n_im = ab_re - 1.0, ab_im
    c_re = (n_re * ar + n_im * ai) / den
    c_im = (n_im * ar - n_re * ai) / den
    br, bi = B_re.astype(f32), B_im.astype(f32)
    bb_re = c_re[..., None] * br - c_im[..., None] * bi
    bb_im = c_re[..., None] * bi + c_im[..., None] * br
    bu_re = jnp.einsum('blgc,gpc->blgp', uf, bb_re)
    bu_im = jnp.einsum('blgc,gpc->blgp', uf, bb_im)
    a_re = jnp.broadcast_to(ab_re, (1, L, SSM_GROUPS, SSM_STATE))
    a_im = jnp.broadcast_to(ab_im, (1, L, SSM_GROUPS, SSM_STATE))
    _, _, xr, xi = lax.associative_scan(_ssm_combine, (a_re, a_im, bu_re, bu_im), axis=1)
    y = (jnp.einsum('blgp,gcp->blgc', xr, C_re.astype(f32))
         - jnp.einsum('blgp,gcp->blgc', xi, C_im.astype(f32))
         + D_skip.astype(f32).reshape(SSM_GROUPS, SSM_GROUP) * uf)
    y = jax.nn.gelu(y.reshape(Bsz, L, SSM_WIDTH)).astype(u.dtype)
    a, g = jnp.split(y @ w_glu, 2, axis=-1)
    return a * jax.nn.sigmoid(g)

def setup_inputs(seed: int = 0) -> dict:
    key = jax.random.key(seed)
    ks = iter(jax.random.split(key, 40))
    f32 = jnp.float32

    def nrm(shape, scale):
        return jax.random.normal(next(ks), shape, f32) * scale

    def gain(shape):
        return 1.0 + 0.05 * jax.random.normal(next(ks), shape, f32)

    x = jax.random.normal(next(ks), (BATCH, SEQ, D_MODEL), f32)
    mem = jax.random.normal(next(ks), (BATCH, MEM_LEN, D_MODEL), f32)
    offsets = jax.random.randint(next(ks), (BATCH, 1), 0, 4096, dtype=jnp.int32)
    positions = (offsets + jnp.arange(SEQ, dtype=jnp.int32)[None, :]).astype(jnp.int32)
    n_idx = jnp.arange(SSM_STATE, dtype=f32)
    ssm_A_re = -0.5 + 0.01 * jax.random.normal(next(ks), (DEPTH, SSM_GROUPS, SSM_STATE), f32)
    ssm_A_im = math.pi * n_idx + 0.01 * jax.random.normal(next(ks), (DEPTH, SSM_GROUPS, SSM_STATE), f32)
    ssm_log_dt = jax.random.uniform(next(ks), (DEPTH, SSM_GROUPS), f32,
                                    math.log(DT_MIN), math.log(DT_MAX))
    return {
        'x': x,
        'mem': mem,
        'positions': positions,
        'g_mix_pre': gain((DEPTH, D_MODEL)),
        'g_mix_post': gain((DEPTH, D_MODEL)),
        'g_mem': gain((DEPTH, D_MODEL)),
        'g_mlp_pre': gain((DEPTH, D_MODEL)),
        'g_mlp_post': gain((DEPTH, D_MODEL)),
        'sinks': nrm((DEPTH, N_Q_HEADS), 0.5),
        'w_in': nrm((DEPTH, D_MODEL, IN_COLS), D_MODEL ** -0.5),
        'w_mem_kv': nrm((DEPTH, D_MODEL, 2 * X_WIDTH), D_MODEL ** -0.5),
        'ssm_A_re': ssm_A_re,
        'ssm_A_im': ssm_A_im,
        'ssm_log_dt': ssm_log_dt,
        'ssm_B_re': nrm((DEPTH, SSM_GROUPS, SSM_STATE, SSM_GROUP), (2 * SSM_GROUP) ** -0.5),
        'ssm_B_im': nrm((DEPTH, SSM_GROUPS, SSM_STATE, SSM_GROUP), (2 * SSM_GROUP) ** -0.5),
        'ssm_C_re': nrm((DEPTH, SSM_GROUPS, SSM_GROUP, SSM_STATE), (2 * SSM_STATE) ** -0.5),
        'ssm_C_im': nrm((DEPTH, SSM_GROUPS, SSM_GROUP, SSM_STATE), (2 * SSM_STATE) ** -0.5),
        'ssm_D': nrm((DEPTH, SSM_WIDTH), 1.0),
        'w_glu': nrm((DEPTH, SSM_WIDTH, 2 * SSM_WIDTH), SSM_WIDTH ** -0.5),
        'w_branch_attn': nrm((DEPTH, ATTN_WIDTH, D_MODEL), ATTN_WIDTH ** -0.5),
        'w_branch_ssm': nrm((DEPTH, SSM_WIDTH, D_MODEL), SSM_WIDTH ** -0.5),
        'w_branch_mem': nrm((DEPTH, X_WIDTH, D_MODEL), X_WIDTH ** -0.5),
        'w_out': nrm((DEPTH, D_MODEL, D_MODEL), D_MODEL ** -0.5),
        'w_up': nrm((DEPTH, D_MODEL, D_FF), D_MODEL ** -0.5),
        'w_down': nrm((DEPTH, D_FF, D_MODEL), D_FF ** -0.5),
    }

def reference(x, mem, positions, g_mix_pre, g_mix_post, g_mem, g_mlp_pre, g_mlp_post,
              sinks, w_in, w_mem_kv, ssm_A_re, ssm_A_im, ssm_log_dt, ssm_B_re, ssm_B_im,
              ssm_C_re, ssm_C_im, ssm_D, w_glu, w_branch_attn, w_branch_ssm, w_branch_mem,
              w_out, w_up, w_down):
    B, L = x.shape[0], x.shape[1]
    for l in range(DEPTH):
        h = rmsnorm(x, g_mix_pre[l])
        z = h @ w_in[l]
        q, k, v, u, qx, gates = jnp.split(z, _IN_SPLITS, axis=-1)
        q = rope(q.reshape(B, L, N_Q_HEADS, HEAD_DIM), positions)
        k = rope(k.reshape(B, L, N_KV_HEADS, HEAD_DIM), positions)
        v = v.reshape(B, L, N_KV_HEADS, HEAD_DIM)
        y_attn = sliding_window_attention(q, k, v, sinks[l])
        y_ssm = s5_branch(u, ssm_A_re[l], ssm_A_im[l], ssm_log_dt[l], ssm_B_re[l],
                          ssm_B_im[l], ssm_C_re[l], ssm_C_im[l], ssm_D[l], w_glu[l])
        mkv = rmsnorm(mem, g_mem[l]) @ w_mem_kv[l]
        km, vm = jnp.split(mkv, 2, axis=-1)
        km = km.reshape(B, MEM_LEN, X_HEADS, X_HEAD_DIM)
        vm = vm.reshape(B, MEM_LEN, X_HEADS, X_HEAD_DIM)
        y_mem = memory_cross_attention(qx, km, vm)
        gt = jax.nn.sigmoid(gates.reshape(B, L, N_BRANCH, D_MODEL))
        merged = (gt[:, :, 0] * (y_attn @ w_branch_attn[l])
                  + gt[:, :, 1] * (y_ssm @ w_branch_ssm[l])
                  + gt[:, :, 2] * (y_mem @ w_branch_mem[l]))
        x = x + rmsnorm(merged @ w_out[l], g_mix_post[l])
        h = rmsnorm(x, g_mlp_pre[l])
        f = jnp.square(jax.nn.relu(h @ w_up[l])) @ w_down[l]
        x = x + rmsnorm(f, g_mlp_post[l])
    return x


_drawn_inputs = setup_inputs


def setup_inputs(seed=0):
    import zlib

    import numpy as np

    out = dict(_drawn_inputs(seed))
    spreads = {}
    factors = {'g_mem': 3.922,
     'sinks': 31.092,
     'ssm_A_re': 200.0,
     'ssm_A_im': 64.0,
     'ssm_log_dt': 64.0,
     'ssm_B_re': 64.0,
     'ssm_B_im': 64.0,
     'ssm_C_re': 64.0,
     'ssm_C_im': 64.0}
    for name, (base, spread) in spreads.items():
        noise = np.random.default_rng([zlib.crc32(name.encode()), seed]).standard_normal(out[name].shape)
        drawn = base * np.exp(spread * noise) if base else spread * noise
        out[name] = __import__('jax').numpy.asarray(drawn.astype(out[name].dtype))
    for name, factor in factors.items():
        out[name] = (out[name] * factor).astype(out[name].dtype)
    return out
```

```python
from contextlib import ExitStack, contextmanager

import numpy as np
import concourse.bass as bass
from concourse import mybir

P = 128
D = 1024
L = 1024
KT = D // P
NT = L // P
MEM = 256
HD = 64
CH = 64
NCH = L // CH
W512 = 512
BT = W512 // P
XH = 4
DFF = 4096
EPS = 1e-6
STEP = 8
NC8 = L // STEP
NPAIR = 16
SG = 16
ST = 64
RP = 4
C_V, C_U, C_QX, C_G = 640, 768, 1280, 1792
UNIT = 2048

U_MEM, U_QX, U_Q, U_KV, U_U, U_GLU, U_MERGE, U_OUT, U_MLP = 0, 4, 6, 8, 9, 11, 13, 31, 35
STAGES = [("front", 28), ("qx", 8), ("xsc", 16), ("q", 8), ("kv", 4), ("xpv", 24), ("rope", 10), ("vwin", 4),
          ("ssc", 16), ("u", 8), ("spv", 24), ("spar", 3), ("s5", 40), ("yg", 8), ("glu", 16),
          ("merge", 96), ("wout", 16), ("h2", 16), ("mlp", 192)]
FIRST = {}
_n = 0
for _name, _count in STAGES:
    FIRST[_name] = _n
    _n += _count

RSQRT_SEED = float(0x5F3759DF)
MAGIC = 12582912.0


def _chunks_of(value, bits, n):
    out = []
    for _ in range(n - 1):
        e = int(np.floor(np.log2(abs(value))))
        c = float(np.floor(value / 2.0 ** (e - bits + 1)) * 2.0 ** (e - bits + 1))
        out.append(c)
        value -= c
    return out + [float(np.float32(value))]


TWO_PI = _chunks_of(2 * np.pi, 8, 4)
LN2 = _chunks_of(np.log(2.0), 12, 2)
PI_DOWN = float(np.float32(3.1415925))


def pv_event(g, part):
    if part < 2:
        return part if g == 0 else 2 + 3 * (g - 1) + part
    return 4 + 3 * g if g < 7 else 23


def hybrid_layer(nc, a, out):
    f32, f32r, i32 = mybir.dt.float32, mybir.dt.float32r, mybir.dt.int32
    ALU, ACT, AX = mybir.AluOpType, mybir.ActivationFunctionType, mybir.AxisListType
    add, sub, mul = ALU.add, ALU.subtract, ALU.mult
    ctx = ExitStack()
    with ctx:
        def sb(name, shape, dt=f32, stack=ctx):
            return stack.enter_context(nc.sbuf_tensor(name, shape, dt))

        def sem(name):
            return ctx.enter_context(nc.semaphore(name))

        @contextmanager
        def overlay():
            with ExitStack() as stack:
                yield lambda name, shape, dt=f32: sb(name, shape, dt, stack)

        ident = sb("ident", [P, P])
        rotm = sb("rotm", [P, P])
        halfpi = sb("halfpi", [P, 1])
        stat = sb("stat", [P, 8])
        sumsq = sb("sumsq", [P, 40])
        mx = sb("mx", [P, 64])
        den = sb("den", [P, 64])
        sinkb = sb("sinkb", [P, 4])
        sinkx = sb("sinkx", [P, 16, 4])
        ldt = sb("ldt", [NPAIR, 2])
        raw = sb("raw", [P, 2, UNIT])
        whi = sb("whi", [P, 2, UNIT], f32r)
        wlo = sb("wlo", [P, 2, UNIT], f32r)
        hThi = sb("hThi", [P, KT, L], f32r)
        hTlo = sb("hTlo", [P, KT, L], f32r)
        yst = sb("yst", [P, 4, 512])
        tok = sb("tok", [P, 4096])
        scr = sb("scr", [P, 2, 512])
        with ExitStack() as att:
            kmT = sb("kmT", [P, XH, MEM], f32, att)
            vm = sb("vm", [P, 2, W512], f32, att)
            kT = sb("kT", [P, L], f32, att)
            vT = sb("vT", [P, L], f32, att)
            with overlay() as ov:
                mThi = ov("mThi", [P, KT, MEM], f32r)
                mTlo = ov("mTlo", [P, KT, MEM], f32r)
                xst = ov("xst", [P, 3, D])
                hst = ov("hst", [P, 2, D])
                gpre = ov("gpre", [P, D])
                gmem = ov("gmem", [P, D])
                junk = ov("junk", [P, D])
            with overlay() as ov:
                prob = ov("prob", [P, 16, 512])
                pT = ov("pT", [P, 2, 2, 512])
                with overlay() as ov2:
                    cosT = ov2("cosT", [P, L])
                    sinT = ov2("sinT", [P, L])
                with overlay() as ov2:
                    vwin = ov2("vwin", [P, NCH, P])
        with overlay() as ov:
            spar = ov("spar", [P, 3, NPAIR])
            sB = ov("sB", [P, 2, NPAIR, SG])
            Bb = ov("Bb", [P, 2, NPAIR, SG])
            cpk = ov("cpk", [P, 2, NPAIR, SG])
            cbd = ov("cbd", [P, 2, NPAIR, 2 * SG])
            pwF = ov("pwF", [P, 2, NPAIR, 9])
            pwR = ov("pwR", [P, 2, NPAIR, 8])
            rotF = ov("rotF", [P, 2, 7, NPAIR])
            rho = ov("rho", [P, NPAIR])
            small = ov("small", [P, 12, NPAIR])
            smalli = ov("smalli", [P, NPAIR], i32)
            Dbc = ov("Dbc", [P, W512])
            Xp = ov("Xp", [P, 2, RP, 15 * SG])
            ca = ov("ca", [P, 2, RP, 256])
            Mt = ov("Mt", [P, 2 * RP, P])
            wT = ov("wT", [P, 2, RP, P])
            uT = ov("uT", [P, 2 * RP, P])
            E = ov("E", [P, 2, RP, NC8])
            v5 = ov("v5", [P, 2, RP, NC8])
            z5 = ov("z5", [P, 2, RP, NC8])
            xs = ov("xs", [P, 2, RP, NC8])
            t1 = ov("t1", [P, 512])
            t2 = ov("t2", [P, 512])
        with overlay() as ov:
            yhi = ov("yhi", [P, BT, L], f32r)
            ylo = ov("ylo", [P, BT, L], f32r)
            acc = ov("acc", [P, KT, L])
        qwin = tok[:, :].rearrange("p (a n h c) -> p a h n c", a=2, n=NCH, h=2)
        qflat = tok[:, :].rearrange("p (a n x) -> p a n x", a=2, n=NCH)
        uc = tok[:, :].rearrange("p (g i c) -> p g i c", g=32, i=STEP)
        gl = [t[:, :, :, :].rearrange("p a b c -> p (a b) c") for t in (E, v5, z5, xs)]
        craw = scr[:, :, :].rearrange("p a (r d x) -> p a r d x", r=4, d=2)
        sload = yst[0:NPAIR, 0, 0:384].rearrange("p (a x) -> p a x", a=3)

        y_dram = nc.dram_tensor("y_scratch", (3, BT, P, L), f32, kind="Internal").ap()
        x1_dram = nc.dram_tensor("x1_scratch", (L, D), f32, kind="Internal").ap()

        banks = [ctx.enter_context(nc.psum_tensor(f"bank{b}", [P, 512], f32)) for b in range(8)]
        bank_full = [sem(f"bank_full{b}") for b in range(8)]
        bank_free = [sem(f"bank_free{b}") for b in range(8)]
        w_loaded = [sem(f"w_loaded{s}") for s in range(2)]
        w_hi, w_lo = sem("w_hi"), sem("w_lo")
        consts = sem("consts")
        gains_in = sem("gains_in")
        pos_in = sem("pos_in")
        sinks_in = sem("sinks_in")
        tile_in = [sem(f"tile_in{s}") for s in range(3)]
        square_sum = sem("square_sum")
        h_made = sem("h_made")
        split_hi = sem("split_hi")
        trig_arg, trig_done = sem("trig_arg"), sem("trig_done")
        x_exp, x_prob = sem("x_exp"), sem("x_prob")
        s_exp, s_prob, sink_arg, sink_exp = sem("s_exp"), sem("s_prob"), sem("sink_arg"), sem("sink_exp")
        rope_done = sem("rope_done")
        y_sent = [sem(f"y_sent{s}") for s in range(4)]
        y_loaded = [sem(f"y_loaded{s}") for s in range(4)]
        y_hi, y_lo = sem("y_hi"), sem("y_lo")
        s5_in = sem("s5_in")
        s5_c, s5_dt = sem("s5_c"), sem("s5_dt")
        s5_trig, s5_trig_done = sem("s5_trig"), sem("s5_trig_done")
        s5_x, s5_ca, s5_xs, s5_du, gelu_done = sem("s5_x"), sem("s5_ca"), sem("s5_xs"), sem("s5_du"), sem("gelu_done")
        acc_zero = sem("acc_zero")
        merge_mul, merged = sem("merge_mul"), sem("merged")
        m_hi, m_lo = sem("m_hi"), sem("m_lo")
        post_gains = sem("post_gains")
        x_back, x1_made, x1_sent, h2_made = [sem("x_back0"), sem("x_back1")], sem("x1_made"), sem("x1_sent"), sem("h2_made")
        sq_o, sq_x = sem("sq_o"), sem("sq_x")
        f_sq, f_hi, f_lo = sem("f_sq"), sem("f_hi"), sem("f_lo")
        acc_done = sem("acc_done")
        last_gain = sem("last_gain")
        x1_back = [sem(f"x1_back{s}") for s in range(3)]
        out_made, out_sent = sem("out_made"), sem("out_sent")
        chain = sem("chain")
        block = ctx.enter_context(nc.Block())

        def wait_free(eng, n, it=0, per=0):
            if n >= 8:
                eng.wait_ge(bank_free[n % 8], n // 8 + it * (per // 8))

        def wait_full(eng, n, it=0, per=0):
            eng.wait_ge(bank_full[n % 8], n // 8 + 1 + it * (per // 8))

        def wait_taken(eng, n, it=0, per=0):
            eng.wait_ge(bank_free[n % 8], n // 8 + 1 + it * (per // 8))

        def prep_hi(act, u, n_before, it=0, per=0, ev=0):
            dmas = 2 * (u // 2 + 1) + (2 if u >= U_Q else 0)
            act.wait_ge(w_loaded[u % 2], 16 * dmas + it * (16 * per))
            if n_before is not None:
                wait_full(act, n_before, it, ev)
            nc.scalar.activation(whi[:, u % 2, :], raw[:, u % 2, :], ACT.Copy).then_inc(w_hi, 1)

        def prep_lo(dve, u, it=0, per=0):
            dve.wait_ge(w_hi, u + 1 + it * per)
            nc.vector.tensor_tensor(wlo[:, u % 2, :], raw[:, u % 2, :], whi[:, u % 2, :].bitcast(f32), sub).then_inc(w_lo, 1)

        def wviews(u, kt):
            w = UNIT // kt
            return (whi[:, u % 2, :].rearrange("p (k c) -> p k c", c=w), wlo[:, u % 2, :].rearrange("p (k c) -> p k c", c=w))

        @block.sync
        def _(sp):
            def load(u, pieces, it=0, per=0):
                if u >= 2:
                    sp.wait_ge(w_lo, u - 1 + it * per)
                for dst, src in pieces:
                    sp.dma_start(dst, src).then_inc(w_loaded[u % 2], 16)

            def cols(u, src, kt=KT):
                v = raw[:, u % 2, :].rearrange("p (k c) -> p k c", k=kt)
                s = src.rearrange("(k p) c -> p k c", p=P)
                h = kt // 2
                return [(v[:, 0:h, :], s[:, 0:h, :]), (v[:, h:kt, :], s[:, h:kt, :])]

            w_in = a["w_in"][0]
            for s in range(4):
                load(U_MEM + s, cols(U_MEM + s, a["w_mem_kv"][0][:, s * 256:(s + 1) * 256]))
            for s in range(2):
                load(U_QX + s, cols(U_QX + s, w_in[:, C_QX + s * 256:C_QX + (s + 1) * 256]))
            for s in range(2):
                u = U_Q + s
                v = raw[:, u % 2, :].rearrange("p (k i j c) -> p k i j c", k=KT, i=2, j=2)
                src = w_in[:, 0:512].rearrange("(k p) (j i c) -> p k i j c", p=P, j=2, c=HD)
                load(u, [(v[:, :, i, j, :], src[:, :, 2 * s + i, j, :]) for i in range(2) for j in range(2)])
            load(U_KV, cols(U_KV, w_in[:, 512:768]))
            for s in range(2):
                load(U_U + s, cols(U_U + s, w_in[:, C_U + s * 256:C_U + (s + 1) * 256]))
            for s in range(2):
                u = U_GLU + s
                v = raw[:, u % 2, :].rearrange("p (k h c) -> p k h c", k=BT, h=2)
                src = a["w_glu"][0].rearrange("(k p) (h c) -> p k h c", p=P, h=2)
                load(u, [(v[:, :, h, :], src[:, :, h, s * 256:(s + 1) * 256]) for h in range(2)])
            for b in range(3):
                wb = a[("w_branch_attn", "w_branch_ssm", "w_branch_mem")[b]][0]
                for s in range(6):
                    u = U_MERGE + 6 * b + s
                    if s % 3 == 0:
                        c0 = (s // 3) * 512
                        v = raw[:, u % 2, :].rearrange("p (k c) -> p k c", k=BT)
                        if b == 0:
                            load(u, [(v[64 * j:64 * j + 64, :, :],
                                      wb[256 * j:256 * j + 256, c0:c0 + 512].rearrange("(k p) c -> p k c", p=HD))
                                     for j in range(2)])
                        else:
                            load(u, cols(u, wb[:, c0:c0 + 512], BT))
                    else:
                        c0 = C_G + b * D + ((s // 3) * 2 + s % 3 - 1) * 256
                        load(u, cols(u, w_in[:, c0:c0 + 256]))
            for s in range(4):
                load(U_OUT + s, cols(U_OUT + s, a["w_out"][0][:, s * 256:(s + 1) * 256]))
            up, down = a["w_up"][0], a["w_down"][0]
            with sp.Fori(0, 8) as it:
                for s in range(2):
                    load(U_MLP + s, cols(U_MLP + s, up[:, bass.ds(it * 512 + s * 256, 256)]), it, 4)
                for s in range(2):
                    load(U_MLP + 2 + s, cols(U_MLP + 2 + s, down[bass.ds(it * 512, 512), s * 512:(s + 1) * 512], BT), it, 4)

        @block.gpsimd
        def _(pool):
            g = nc.gpsimd
            g.memset(ident[:, :], 0.0).then_inc(consts, 1)
            g.memset(rotm[:, :], 0.0).then_inc(consts, 1)
            g.memset(halfpi[:, :], float(np.float32(np.pi / 2))).then_inc(consts, 1)
            pool.wait_ge(consts, 3)
            g.affine_select(out=ident[:, :], in_=ident[:, :], compare_op=ALU.not_equal, fill=1.0, base=0,
                            pattern=[[-1, P]], channel_multiplier=1).then_inc(consts, 1)
            rv = rotm[:, :].rearrange("p (b h c) -> p b h c", b=2, h=2)
            for h, fill, base in ((0, -1.0, -32), (1, 1.0, 0)):
                g.affine_select(out=rv[:, :, h, :], in_=rv[:, :, h, :], compare_op=ALU.not_equal, fill=fill, base=base,
                                pattern=[[-64, 2], [-1, 32]], channel_multiplier=1).then_inc(consts, 1)
            g.dma_start(gmem[:, :], a["g_mem"][0].partition_broadcast(P)).then_inc(gains_in, 16)
            mem, x = a["mem"][0], a["x"][0]
            for idx in range(10):
                if idx >= 3:
                    pool.wait_ge(h_made, idx - 2)
                src = mem[idx * P:(idx + 1) * P, :] if idx < 2 else x[(idx - 2) * P:(idx - 1) * P, :]
                g.dma_start(xst[:, idx % 3, :], src).then_inc(tile_in[idx % 3], 16)
                if idx == 1:
                    g.dma_start(gpre[:, :], a["g_mix_pre"][0].partition_broadcast(P)).then_inc(gains_in, 16)
            g.dma_start(yst[:, 0:2, :].rearrange("p a b -> p (a b)").bitcast(i32),
                        a["positions"][0].partition_broadcast(P)).then_inc(pos_in, 16)
            g.dma_start(stat[:, 7:8], a["inv_freq"]).then_inc(pos_in, 16)
            sk = a["sinks"][0].rearrange("(c h) -> h c", h=2)
            for h in range(2):
                g.dma_start(sinkb[64 * h:64 * h + 64, :], sk[h].partition_broadcast(64), allow_slow_non_contiguous=True).then_inc(sinks_in, 16)
            sent = 0
            for q in range(8):
                wait_taken(pool, FIRST["xpv"] + pv_event(q, 2))
                g.dma_start(y_dram[2, q // 2, :, (q % 2) * 512:(q % 2) * 512 + 512], yst[:, sent % 4, :]).then_inc(y_sent[sent % 4], 16)
                sent += 1
            for q in range(8):
                wait_taken(pool, FIRST["spv"] + pv_event(q, 2))
                g.dma_start(y_dram[0, :, :, q * P:(q + 1) * P].rearrange("i p t -> p i t"),
                            yst[:, sent % 4, :].rearrange("p (i t) -> p i t", i=4)).then_inc(y_sent[sent % 4], 16)
                sent += 1
            for s in range(4):
                pool.wait_ge(y_sent[s], 64)
            for k, name in enumerate(("ssm_A_re", "ssm_A_im")):
                g.dma_start(sload[:, k, :], a[name][0].rearrange("(k g) p -> k (g p)", g=2)).then_inc(s5_in, 16)
            g.dma_start(ldt[:, :], a["ssm_log_dt"][0].rearrange("(k g) -> k g", g=2)).then_inc(s5_in, 16)
            for k, name in enumerate(("ssm_C_re", "ssm_C_im")):
                for d in range(2):
                    g.dma_start(craw[:, k, :, d, :], a[name][0].rearrange("(r g) o p -> (g o) r p", r=4)).then_inc(s5_in, 16)
            for k, name in enumerate(("ssm_B_re", "ssm_B_im")):
                g.dma_start(sB[:, k, :, :], a[name][0].rearrange("(k g) p c -> (g p) k c", g=2)).then_inc(s5_in, 16)
            g.dma_start(Dbc[:, :], a["ssm_D"][0].partition_broadcast(P)).then_inc(s5_in, 16)
            pool.wait_ge(s5_in, 160)
            for r in range(4):
                for e in range(2):
                    wait_taken(pool, FIRST["s5"] + 10 * r + e)
                sl = uc[:, 8 * r:8 * r + 8, :, :]
                dd = Dbc[:, P * r:P * r + P].rearrange("p (g c) -> p g c", c=SG).unsqueeze(2).to_broadcast([P, 8, STEP, SG])
                g.tensor_tensor(sl, sl, dd, mul).then_inc(s5_du, 1)
            for e in range(8):
                wait_full(pool, FIRST["yg"] + e)
            g.memset(acc[:, :, :], 0.0).then_inc(acc_zero, 1)
            for q in range(8):
                wait_taken(pool, FIRST["glu"] + 2 * q)
                g.dma_start(y_dram[1, q // 2, :, (q % 2) * 512:(q % 2) * 512 + 512], yst[:, sent % 4, :]).then_inc(y_sent[sent % 4], 16)
                sent += 1
            for s in range(4):
                pool.wait_ge(y_sent[s], 96)
            with pool.Fori(0, 3) as b:
                for pc in range(8):
                    half, k = pc // 4, pc % 4
                    if pc < 4:
                        pool.wait_ge(y_lo, b * 8 + 1)
                    else:
                        pool.wait_ge(y_lo, b * 8 + pc - 2)
                    g.dma_start(yst[:, k, :], y_dram[bass.ds(b, 1), k, :, half * 512:half * 512 + 512].rearrange("b p t -> (b p) t")).then_inc(y_loaded[k], 16)
            pool.wait_ge(merged, 49)
            g.dma_start(tok[:, 0:D], a["g_mix_post"][0].partition_broadcast(P)).then_inc(post_gains, 16)
            g.dma_start(tok[:, D:2 * D], a["g_mlp_pre"][0].partition_broadcast(P)).then_inc(post_gains, 16)
            yx = yst[:, :, :].rearrange("p (s a) c -> p s (a c)", s=2)
            pool.wait_ge(y_lo, 25)

            def x_load(t):
                g.dma_start(yx[:, t % 2, :], x[t * P:(t + 1) * P, :]).then_inc(x_back[t % 2], 16)

            x_load(0)
            x_load(1)
            for t in range(NT):
                pool.wait_ge(x1_made, t + 1)
                g.dma_start(x1_dram[t * P:(t + 1) * P, :], yx[:, t % 2, :]).then_inc(x1_sent, 16)
                if t + 2 < NT:
                    pool.wait_ge(x1_sent, 16 * (t + 1))
                    pool.wait_ge(h2_made, t + 1)
                    x_load(t + 2)
            pool.wait_ge(x1_sent, 16 * NT)
            g.memset(acc[:, :, :], 0.0).then_inc(acc_zero, 1)
            pool.wait_ge(h2_made, NT)
            for e in range(2):
                wait_taken(pool, FIRST["h2"] + 14 + e)
            g.dma_start(tok[:, 0:D], a["g_mlp_post"][0].partition_broadcast(P)).then_inc(last_gain, 16)

            def x1_load(t):
                g.dma_start(tok[:, (1 + t % 3) * D:(2 + t % 3) * D], x1_dram[t * P:(t + 1) * P, :]).then_inc(x1_back[t % 3], 16)

            for t in range(3):
                x1_load(t)
            for t in range(NT):
                pool.wait_ge(out_made, t + 1)
                g.dma_start(out[0, t * P:(t + 1) * P, :], tok[:, (1 + t % 3) * D:(2 + t % 3) * D]).then_inc(out_sent, 16)
                if t + 3 < NT:
                    pool.wait_ge(out_sent, 16 * (t + 1))
                    x1_load(t + 3)
            pool.wait_ge(out_sent, 16 * NT)

        @block.scalar
        def _(act):
            A = nc.scalar

            def copy_out(n, dst, src=None):
                wait_full(act, n)
                A.activation(dst, banks[n % 8][:, :] if src is None else src, ACT.Copy).then_inc(bank_free[n % 8], 1)

            def square(idx):
                act.wait_ge(tile_in[idx % 3], 16 * (idx // 3 + 1))
                if idx:
                    act.wait_ge(square_sum, idx)
                A.activation(junk[:, :], xst[:, idx % 3, :], ACT.Square, accum_out=sumsq[:, idx:idx + 1]).then_inc(square_sum, 1)

            def norm_event(idx, e):
                return FIRST["front"] + (2 * idx + e if idx < 2 else 6 + 6 * ((idx - 2) // 2) + 2 * ((idx - 2) % 2) + e)

            def norm_hi(idx):
                for e in range(2):
                    n = norm_event(idx, e)
                    dst = (mThi[:, 4 * e:4 * e + 4, idx * P:(idx + 1) * P] if idx < 2
                           else hThi[:, 4 * e:4 * e + 4, (idx - 2) * P:(idx - 1) * P])
                    wait_full(act, n)
                    A.activation(dst, banks[n % 8][:, :].rearrange("p (k t) -> p k t", k=4), ACT.Copy).then_inc(split_hi, 1)

            for idx in range(3):
                square(idx)
            prep_hi(act, 0, None)
            norm_hi(0)
            norm_hi(1)
            for s in range(4):
                n0 = FIRST["front"] + 4 + 6 * s
                prep_hi(act, s + 1, n0 - 1)
                for i in range(2):
                    dst = kmT[:, 2 * s + i, :] if s < 2 else vm[:, i, (s - 2) * 256:(s - 1) * 256]
                    copy_out(n0 + i, dst, banks[(n0 + i) % 8][:, 0:256])
                for idx in (2 + 2 * s, 3 + 2 * s):
                    if idx + 1 < 10:
                        square(idx + 1)
                    norm_hi(idx)
            tokq = tok[:, :].rearrange("p (i t) -> p i t", i=4)
            act.wait_ge(trig_arg, 1)
            act.wait_ge(consts, 6)
            A.activation(cosT[:, :], cosT[:, :], ACT.Sin, scale=-1.0, bias=halfpi[:, 0:1]).then_inc(trig_done, 1)
            A.activation(sinT[:, :], sinT[:, :], ACT.Sin).then_inc(trig_done, 1)
            for s in range(2):
                n0 = FIRST["qx"] + 4 * s
                prep_hi(act, U_QX + s + 1, n0 - 1)
                for i in range(2):
                    for half in range(2):
                        copy_out(n0 + 2 * i + half, tokq[:, 2 * s + i, half * 512:half * 512 + 512])
            for e in range(16):
                wait_taken(act, FIRST["xsc"] + e)
                A.activation(prob[:, e, :], prob[:, e, :], ACT.Exp).then_inc(x_exp, 1)
            for s in range(2):
                n0 = FIRST["q"] + 4 * s
                prep_hi(act, U_Q + s + 1, n0 - 1)
                for i in range(2):
                    for half in range(2):
                        n = n0 + 2 * i + half
                        copy_out(n, qwin[:, s, i, 8 * half:8 * half + 8, :], banks[n % 8][:, :].rearrange("p (n c) -> p n c", c=CH))
            n0 = FIRST["kv"]
            prep_hi(act, U_KV + 1, n0 - 1)
            for i, dst in enumerate((kT, vT)):
                for half in range(2):
                    copy_out(n0 + 2 * i + half, dst[:, half * 512:half * 512 + 512])
            for q in range(8):
                for m in range(2):
                    copy_out(FIRST["xpv"] + pv_event(q, m), pT[:, q % 2, m, :])
            act.wait_ge(rope_done, 10)
            for e in range(4):
                copy_out(FIRST["vwin"] + e, vwin[:, 4 * e:4 * e + 4, :].rearrange("p n d -> p (n d)"))
            for e in range(16):
                act.wait_ge(sink_arg, e + 1)
                pe4 = prob[:, e, :].rearrange("p (s k) -> p s k", s=4)
                if e < 2:
                    A.activation(pe4[:, 0:2, 0:64], pe4[:, 0:2, 0:64], ACT.Exp)
                    A.activation(pe4[:, 2:4, :], pe4[:, 2:4, :], ACT.Exp).then_inc(s_exp, 1)
                else:
                    A.activation(prob[:, e, :], prob[:, e, :], ACT.Exp).then_inc(s_exp, 1)
            A.activation(sinkx[:, :, :], sinkx[:, :, :], ACT.Exp).then_inc(sink_exp, 1)
            for s in range(2):
                n0 = FIRST["u"] + 4 * s
                prep_hi(act, U_U + s + 1, n0 - 1)
                for jj in range(4):
                    n = n0 + jj
                    src = banks[n % 8][:, :].rearrange("p (j g c) -> p j g c", j=2, c=SG)
                    copy_out(n, uc[:, 16 * s:16 * s + 16, 2 * jj:2 * jj + 2, :].rearrange("p g j c -> p j g c"), src)
            for q in range(8):
                for nn in range(2):
                    n = FIRST["spv"] + pv_event(q, nn)
                    nk = 64 if q == 0 and nn == 0 else P
                    copy_out(n, pT[0:nk, q % 2, nn, :], banks[n % 8][0:nk, :])
            act.wait_ge(s5_in, 160)
            A.activation(sload[:, 2, :].rearrange("k (g p) -> k g p", g=2), ldt[:, :].unsqueeze(2).to_broadcast([NPAIR, 2, ST]),
                         ACT.Copy).then_inc(s5_dt, 1)
            n = FIRST["spar"]
            copy_out(n, spar[:, :, :].rearrange("p a b -> p (a b)"), banks[n % 8][:, 0:48])
            for ri in range(2):
                n = FIRST["spar"] + 1 + ri
                wait_full(act, n)
                src = banks[n % 8][:, :].rearrange("p (k g o) -> p g k o", g=2, o=SG)
                A.activation(cpk[0:64, ri, :, :], src[0:64, 0, :, :], ACT.Copy)
                A.activation(cpk[64:P, ri, :, :], src[64:P, 1, :, :], ACT.Copy).then_inc(bank_free[n % 8], 1)
            act.wait_ge(s5_trig, 1)
            A.activation(small[:, 5, :], small[:, 5, :], ACT.Sin, scale=-1.0, bias=halfpi[:, 0:1]).then_inc(s5_trig_done, 1)
            A.activation(small[:, 4, :], small[:, 4, :], ACT.Sin).then_inc(s5_trig_done, 1)
            for r in range(4):
                n0 = FIRST["s5"] + 10 * r
                for e in range(2):
                    copy_out(n0 + e, uT[:, 4 * e:4 * e + 4, :].rearrange("p g c -> p (g c)"))
                for ri in range(2):
                    copy_out(n0 + 2 + ri, wT[:, ri, :, :].rearrange("p g c -> p (g c)"))
                for e in range(2):
                    n = n0 + 4 + e
                    wait_full(act, n)
                    for pp in range(2):
                        pr = 2 * e + pp
                        src = banks[n % 8][:, pp * 256:pp * 256 + 256].rearrange("p (i g o) -> p g i o", g=2, o=SG)
                        ins = A.activation(Mt[:, 2 * pr:2 * pr + 2, :].rearrange("p g (i o) -> p g i o", o=SG), src, ACT.Copy)
                    ins.then_inc(bank_free[n % 8], 1)
            for r in range(4):
                for e in range(2):
                    wait_taken(act, FIRST["s5"] + 10 * r + 8 + e)
            for r in range(4):
                A.activation(gl[r].rearrange("p i (g c) -> p g i c", c=SG), uc[:, 8 * r:8 * r + 8, :, :],
                             ACT.Gelu_apprx_tanh).then_inc(gelu_done, 1)
            for e in range(8):
                n = FIRST["yg"] + e
                dst = yhi[:, e // 2, :].rearrange("p (c i) -> p i c", i=STEP)[:, 4 * (e % 2):4 * (e % 2) + 4, :]
                wait_full(act, n)
                A.activation(dst, banks[n % 8][:, :].rearrange("p (i c) -> p i c", i=4), ACT.Copy).then_inc(split_hi, 1)
            for s in range(2):
                n0 = FIRST["glu"] + 8 * s
                prep_hi(act, U_GLU + s + 1, n0 - 1)
                for j in range(4):
                    n = n0 + 2 * j + 1
                    if 4 * s + j >= 2:
                        wait_taken(act, n - 5)
                    wait_full(act, n)
                    A.activation(scr[:, j % 2, :], banks[n % 8][:, :], ACT.Sigmoid).then_inc(bank_free[n % 8], 1)
            with act.Fori(0, 3) as b:
                for pc in range(8):
                    half, k = pc // 4, pc % 4
                    act.wait_ge(y_loaded[k], 32 * b + 16 * (half + 1))
                    A.activation(yhi[:, k, half * 512:half * 512 + 512], yst[:, k, :], ACT.Copy).then_inc(y_hi, 1)
                for s in range(6):
                    n0 = FIRST["merge"] + (0, 8, 12, 16, 24, 28)[s]
                    prep_hi(act, U_MERGE + s + 1, n0 - 1, b, 6, 32)
                    if s % 3 == 0:
                        act.wait_ge(merged, b * 16 + 8 * (s // 3) + 1)
                        for j in range(8):
                            n = n0 + j
                            wait_full(act, n, b, 32)
                            A.activation(tokq[:, j // 2, (j % 2) * 512:(j % 2) * 512 + 512], banks[n % 8][:, :], ACT.Copy).then_inc(bank_free[n % 8], 1)
                    else:
                        for j in range(4):
                            n = n0 + j
                            loc = ((s // 3) * 2 + s % 3 - 1) * 4 + j
                            act.wait_ge(merge_mul, b * 16 + (loc - 1 if loc >= 2 else 0) + 1)
                            wait_full(act, n, b, 32)
                            A.activation(scr[:, j % 2, :], banks[n % 8][:, :], ACT.Sigmoid).then_inc(bank_free[n % 8], 1)
            act.wait_ge(merged, 49)
            for k in range(KT):
                A.activation(hThi[:, k, :], acc[:, k, :], ACT.Copy).then_inc(m_hi, 1)
            for s in range(4):
                n0 = FIRST["wout"] + 4 * s
                prep_hi(act, U_OUT + s + 1, n0 - 1)
                for j in range(4):
                    n = n0 + j
                    copy_out(n, acc[:, 2 * j:2 * j + 2, s * 256:s * 256 + 256], banks[n % 8][:, :].rearrange("p (t c) -> p t c", t=2))
            yx = yst[:, :, :].rearrange("p (s a) c -> p s (a c)", s=2)
            flat = scr[:, :, :].rearrange("p a c -> p (a c)")

            squares = {"o": 0, "x": 0}

            def square2(kind, src, column):
                if squares["o"]:
                    act.wait_ge(sq_o, squares["o"])
                if squares["x"]:
                    act.wait_ge(sq_x, squares["x"])
                squares[kind] += 1
                A.activation(flat, src, ACT.Square, accum_out=sumsq[:, column:column + 1]).then_inc(sq_o if kind == "o" else sq_x, 1)

            def square_o(t):
                square2("o", acc[:, t, :], 10 + t)

            def h2_hi(t):
                for e in range(2):
                    n = FIRST["h2"] + 2 * t + e
                    wait_full(act, n)
                    A.activation(hThi[:, 4 * e:4 * e + 4, t * P:(t + 1) * P],
                                 banks[n % 8][:, :].rearrange("p (k t) -> p k t", k=4), ACT.Copy).then_inc(split_hi, 1)

            for j in range(4):
                wait_taken(act, FIRST["wout"] + 12 + j)
            square_o(0)
            square_o(1)
            for t in range(NT):
                act.wait_ge(x1_made, t + 1)
                square2("x", yx[:, t % 2, :], 18 + t)
                if t + 2 < NT:
                    square_o(t + 2)
                if t:
                    h2_hi(t - 1)
            h2_hi(NT - 1)

            def mlp(it, last):
                for s in range(2):
                    n0 = FIRST["mlp"] + 4 * s
                    prep_hi(act, U_MLP + s + 1, n0 - 1, it, 4, 24)
                    for j in range(4):
                        n, pc = n0 + j, 4 * s + j
                        wait_full(act, n, it, 24)
                        A.activation(scr[:, pc % 2, :], banks[n % 8][:, :], ACT.Relu).then_inc(bank_free[n % 8], 1)
                        act.wait_ge(f_sq, it * 8 + pc + 1)
                        A.activation(yhi[:, 2 * s + j // 2, (j % 2) * 512:(j % 2) * 512 + 512], yst[:, pc % 4, :],
                                     ACT.Copy).then_inc(f_hi, 1)
                for s in range(2):
                    n0 = FIRST["mlp"] + 8 + 8 * s
                    if not (last and s == 1):
                        prep_hi(act, U_MLP + 2 + s + 1, n0 - 1, it, 4, 24)

            with act.Fori(0, 7) as it:
                mlp(it, False)
            mlp(7, True)
            for t in range(NT):
                act.wait_ge(acc_done, t + 1)
                square2("o", acc[:, t, :], 26 + t)

        @block.vector
        def _(dve):
            V = nc.vector
            issued = [0]

            def mark(ins):
                issued[0] += 1
                ins.then_inc(chain, 1)

            def settle():
                dve.wait_ge(chain, issued[0])

            def do(ins):
                mark(ins)
                settle()

            def rstd(src):
                do(V.tensor_scalar(stat[:, 0:1], src, 1.0 / D, EPS, mul, add))
                do(V.tensor_scalar(stat[:, 1:2].bitcast(i32), stat[:, 0:1].bitcast(i32), -0.5, RSQRT_SEED, mul, add))
                for _ in range(3):
                    do(V.scalar_tensor_tensor(out=stat[:, 2:3], in0=stat[:, 1:2], scalar=stat[:, 0:1], in1=stat[:, 1:2], op0=mul, op1=mul))
                    do(V.tensor_scalar(stat[:, 2:3], stat[:, 2:3], -0.5, 1.5, mul, add))
                    do(V.tensor_tensor(stat[:, 1:2], stat[:, 1:2], stat[:, 2:3], mul))

            def reduce_angle(x, k):
                do(V.tensor_scalar(k, x, float(np.float32(1 / (2 * np.pi))), MAGIC, mul, add))
                do(V.tensor_scalar(k, k, MAGIC, None, sub))
                for c in TWO_PI:
                    do(V.scalar_tensor_tensor(out=x, in0=k, scalar=-c, in1=x, op0=mul, op1=add))
                do(V.tensor_scalar(x, x, PI_DOWN, -PI_DOWN, ALU.min, ALU.max))
                do(V.scalar_tensor_tensor(out=k, in0=x, scalar=-1.0, in1=x, op0=mul, op1=ALU.max))

            def cmul(o, x, y, t):
                mark(V.tensor_tensor(t[0], x[0], y[0], mul))
                mark(V.tensor_tensor(t[1], x[1], y[1], mul))
                settle()
                do(V.tensor_tensor(o[0], t[0], t[1], sub))
                mark(V.tensor_tensor(t[0], x[0], y[1], mul))
                mark(V.tensor_tensor(t[1], x[1], y[0], mul))
                settle()
                do(V.tensor_tensor(o[1], t[0], t[1], add))

            def norm_event(idx, e):
                return FIRST["front"] + (2 * idx + e if idx < 2 else 6 + 6 * ((idx - 2) // 2) + 2 * ((idx - 2) % 2) + e)

            def norm_h(idx):
                dve.wait_ge(square_sum, idx + 1)
                rstd(sumsq[:, idx:idx + 1])
                if idx in (0, 2):
                    dve.wait_ge(gains_in, 16 if idx == 0 else 32)
                V.scalar_tensor_tensor(out=hst[:, idx % 2, :], in0=xst[:, idx % 3, :], scalar=stat[:, 1:2],
                                       in1=(gmem if idx < 2 else gpre)[:, :], op0=mul, op1=mul).then_inc(h_made, 1)

            def norm_lo(idx):
                for e in range(2):
                    n = norm_event(idx, e)
                    sl = (slice(None), slice(4 * e, 4 * e + 4), slice((idx % 2) * P, (idx % 2) * P + P) if idx < 2
                          else slice((idx - 2) * P, (idx - 1) * P))
                    hi, lo = (mThi, mTlo) if idx < 2 else (hThi, hTlo)
                    dve.wait_ge(split_hi, 2 * idx + e + 1)
                    V.tensor_tensor(lo[sl], banks[n % 8][:, :].rearrange("p (k t) -> p k t", k=4), hi[sl].bitcast(f32), sub)\
                        .then_inc(bank_free[n % 8], 1)

            norm_h(0)
            norm_h(1)
            prep_lo(dve, 0)
            norm_lo(0)
            norm_lo(1)
            norm_h(2)
            for s in range(4):
                prep_lo(dve, s + 1)
                for idx in (2 + 2 * s, 3 + 2 * s):
                    if idx + 1 < 10:
                        norm_h(idx + 1)
                    norm_lo(idx)
            dve.wait_ge(pos_in, 32)
            dve.wait_ge(h_made, 10)
            do(V.tensor_scalar(sinT[:, :], yst[:, 0:2, :].rearrange("p a b -> p (a b)").bitcast(i32), stat[:, 7:8], None, mul))
            reduce_angle(sinT[:, :], cosT[:, :])
            dve.sem_inc(trig_arg, 1)
            prep_lo(dve, U_QX + 1)
            prep_lo(dve, U_QX + 2)
            XS = float(P) ** -0.5
            for e in range(16):
                n = FIRST["xsc"] + e
                ps = banks[n % 8][:, :].rearrange("p (h m) -> p h m", h=2)
                wait_full(dve, n)
                m2 = mx[:, 2 * e:2 * e + 2]
                do(V.reduce_max(m2, ps, AX.X))
                do(V.tensor_scalar(m2, m2, XS, None, mul))
                V.scalar_tensor_tensor(out=prob[:, e, :].rearrange("p (h m) -> p h m", h=2), in0=ps, scalar=XS,
                                       in1=m2.unsqueeze(2).to_broadcast([P, 2, MEM]), op0=mul, op1=sub).then_inc(bank_free[n % 8], 1)

            def x_normalise(e):
                pe2 = prob[:, e, :].rearrange("p (h m) -> p h m", h=2)
                d2 = den[:, 2 * e:2 * e + 2]
                dve.wait_ge(x_exp, e + 1)
                do(V.reduce_sum(d2, pe2, AX.X))
                do(V.reciprocal(d2, d2))
                V.tensor_tensor(pe2, pe2, d2.unsqueeze(2).to_broadcast([P, 2, MEM]), mul).then_inc(x_prob, 1)

            prep_lo(dve, U_Q + 1)
            for e in range(8):
                x_normalise(e)
            prep_lo(dve, U_Q + 2)
            for e in range(8, 16):
                x_normalise(e)
            prep_lo(dve, U_KV + 1)
            sent = 0
            for q in range(8):
                n = FIRST["xpv"] + pv_event(q, 2)
                wait_full(dve, n)
                if sent >= 4:
                    dve.wait_ge(y_sent[sent % 4], 16 * (sent // 4))
                V.tensor_copy(yst[:, sent % 4, :], banks[n % 8][:, :]).then_inc(bank_free[n % 8], 1)
                sent += 1
            dve.wait_ge(trig_done, 2)
            for e in range(10):
                n = FIRST["rope"] + e
                half = slice((e % 2) * 512, (e % 2) * 512 + 512)
                by_chunk = lambda v: v.rearrange("p (n c) -> p n c", c=CH)
                qk = qwin[:, e // 4, (e // 2) % 2, 8 * (e % 2):8 * (e % 2) + 8, :] if e < 8 else by_chunk(kT[:, half])
                wait_full(dve, n)
                mark(V.tensor_tensor(scr[:, e % 2, :], banks[n % 8][:, :], sinT[:, half], mul))
                mark(V.tensor_tensor(qk, qk, by_chunk(cosT[:, half]), mul))
                settle()
                V.tensor_tensor(qk, qk, by_chunk(scr[:, e % 2, :]), add).then_inc(rope_done, 1)
                dve.sem_inc(bank_free[n % 8], 1)
            SS = float(HD) ** -0.5
            dve.wait_ge(sinks_in, 32)
            for e in range(16):
                n = FIRST["ssc"] + e
                j = e % 2
                ps = banks[n % 8][:, :].rearrange("p (s k) -> p s k", s=4)
                pe4 = prob[:, e, :].rearrange("p (s k) -> p s k", s=4)
                parts = [(0, 2, 64), (2, 4, P)] if e < 2 else [(0, 4, P)]
                m4 = mx[:, 4 * e:4 * e + 4]
                wait_full(dve, n)
                for lo, hi, nk in parts:
                    mark(V.reduce_max(m4[:, lo:hi], ps[:, lo:hi, 0:nk], AX.X))
                settle()
                sk = sinkb[:, 2 * j:2 * j + 2].unsqueeze(1).to_broadcast([P, 2, 2])
                do(V.scalar_tensor_tensor(out=m4.rearrange("p (s a) -> p s a", s=2), in0=m4.rearrange("p (s a) -> p s a", s=2),
                                          scalar=SS, in1=sk, op0=mul, op1=ALU.max))
                for lo, hi, nk in parts:
                    ins = V.scalar_tensor_tensor(out=pe4[:, lo:hi, 0:nk], in0=ps[:, lo:hi, 0:nk], scalar=SS,
                                                 in1=m4[:, lo:hi].unsqueeze(2).to_broadcast([P, hi - lo, nk]), op0=mul, op1=sub)
                ins.then_inc(bank_free[n % 8], 1)
                V.tensor_tensor(sinkx[:, e, :].rearrange("p (s a) -> p s a", s=2), sk,
                                m4.rearrange("p (s a) -> p s a", s=2), sub).then_inc(sink_arg, 1)

            def s_normalise(e):
                pe4 = prob[:, e, :].rearrange("p (s k) -> p s k", s=4)
                parts = [(0, 2, 64), (2, 4, P)] if e < 2 else [(0, 4, P)]
                d4 = den[:, 4 * e:4 * e + 4]
                for lo, hi, nk in parts:
                    mark(V.reduce_sum(d4[:, lo:hi], pe4[:, lo:hi, 0:nk], AX.X))
                settle()
                do(V.tensor_tensor(d4, d4, sinkx[:, e, :], add))
                do(V.reciprocal(d4, d4))
                for lo, hi, nk in parts:
                    ins = V.tensor_tensor(pe4[:, lo:hi, 0:nk], pe4[:, lo:hi, 0:nk],
                                          d4[:, lo:hi].unsqueeze(2).to_broadcast([P, hi - lo, nk]), mul)
                ins.then_inc(s_prob, 1)

            dve.wait_ge(sink_exp, 1)
            prep_lo(dve, U_U + 1)
            for e in range(16):
                s_normalise(e)
            prep_lo(dve, U_U + 2)
            for q in range(8):
                n = FIRST["spv"] + pv_event(q, 2)
                wait_full(dve, n)
                dve.wait_ge(y_sent[sent % 4], 16 * (sent // 4))
                V.tensor_copy(yst[:, sent % 4, :].rearrange("p (i s t) -> p s i t", i=4, s=2),
                              banks[n % 8][:, :].rearrange("p (s i t) -> p s i t", s=2, i=4)).then_inc(bank_free[n % 8], 1)
                sent += 1

            sm = [small[:, k, :] for k in range(12)]

            def exp_exact(o, x, t):
                k, r, pw = t
                do(V.tensor_scalar(r, x, 200.0, -200.0, ALU.min, ALU.max))
                do(V.tensor_scalar(k, r, float(np.float32(1 / np.log(2.0))), MAGIC, mul, add))
                do(V.tensor_scalar(k, k, MAGIC, None, sub))
                do(V.tensor_scalar(k, k, 128.0, -127.0, ALU.min, ALU.max))
                for c in LN2:
                    do(V.scalar_tensor_tensor(out=r, in0=k, scalar=-c, in1=r, op0=mul, op1=add))
                do(V.tensor_scalar(smalli[:, :], k, 127.0, 8388608.0, add, mul))
                fact = [1.0]
                for q in range(1, 8):
                    fact.append(fact[-1] * q)
                do(V.tensor_scalar(pw, r, 1.0 / fact[7], None, mul))
                for q in range(6, 0, -1):
                    do(V.scalar_tensor_tensor(out=pw, in0=pw, scalar=1.0 / fact[q], in1=r, op0=add, op1=mul))
                do(V.scalar_tensor_tensor(out=o, in0=pw, scalar=1.0, in1=smalli[:, :].bitcast(f32), op0=add, op1=mul))

            for e in range(3):
                wait_taken(dve, FIRST["spar"] + e)
            dve.wait_ge(s5_in, 160)
            a_re, a_im, log_dt = spar[:, 0, :], spar[:, 1, :], spar[:, 2, :]
            exp_exact(sm[0], log_dt, sm[1:4])
            do(V.tensor_tensor(sm[4], a_im, sm[0], mul))
            do(V.tensor_tensor(sm[6], a_re, sm[0], mul))
            reduce_angle(sm[4], sm[5])
            dve.sem_inc(s5_trig, 1)
            exp_exact(sm[6], sm[6], sm[1:4])
            dve.wait_ge(s5_trig_done, 2)
            sin, cos, mag = sm[4], sm[5], sm[6]
            do(V.memset(pwF[:, 0, :, 0:1], 1.0))
            do(V.memset(pwF[:, 1, :, 0:1], 0.0))
            do(V.tensor_tensor(pwF[:, 0, :, 1], mag, cos, mul))
            do(V.tensor_tensor(pwF[:, 1, :, 1], mag, sin, mul))
            for k in (1, 2, 4):
                o = [pwF[:, ri, :, k + 1:2 * k + 1] for ri in range(2)]
                x = [pwF[:, ri, :, 1:k + 1] for ri in range(2)]
                y = [pwF[:, ri, :, k].unsqueeze(2).to_broadcast([P, NPAIR, k]) for ri in range(2)]
                t = [tt[:, 0:NPAIR * k].rearrange("p (a b) -> p a b", b=k) for tt in (t1, t2)]
                cmul(o, x, y, t)
            for j in range(8):
                mark(V.tensor_copy(pwR[:, :, :, j], pwF[:, :, :, 7 - j]))
            settle()
            do(V.tensor_tensor(sm[1], a_re, a_re, mul))
            do(V.tensor_tensor(sm[2], a_im, a_im, mul))
            do(V.tensor_tensor(sm[1], sm[1], sm[2], add))
            do(V.reciprocal(sm[1], sm[1]))
            do(V.tensor_scalar(sm[2], pwF[:, 0, :, 1], 1.0, None, sub))
            n_im = pwF[:, 1, :, 1]
            do(V.tensor_tensor(sm[7], sm[2], a_re, mul))
            do(V.tensor_tensor(sm[8], n_im, a_im, mul))
            do(V.tensor_tensor(sm[7], sm[7], sm[8], add))
            do(V.tensor_tensor(sm[7], sm[7], sm[1], mul))
            do(V.tensor_tensor(sm[8], n_im, a_re, mul))
            do(V.tensor_tensor(sm[9], sm[2], a_im, mul))
            do(V.tensor_tensor(sm[8], sm[8], sm[9], sub))
            do(V.tensor_tensor(sm[8], sm[8], sm[1], mul))
            t256 = [tt[:, 0:256].rearrange("p (a b) -> p a b", b=SG) for tt in (t1, t2)]
            cmul([Bb[:, ri, :, :] for ri in range(2)], [sm[7 + ri].unsqueeze(2).to_broadcast([P, NPAIR, SG]) for ri in range(2)],
                 [sB[:, ri, :, :] for ri in range(2)], t256)
            do(V.memset(cbd[:, :, :, :], 0.0))
            do(V.memset(ca[:, :, :, :], 0.0))
            do(V.memset(Xp[:, :, :, P:15 * SG], 0.0))
            do(V.memset(xs[:, :, :, 0:1], 0.0))
            for gg in range(2):
                s = slice(64 * gg, 64 * gg + 64)
                mark(V.tensor_copy(cbd[s, 0, :, gg * SG:gg * SG + SG], cpk[s, 0, :, :]))
                mark(V.tensor_scalar(cbd[s, 1, :, gg * SG:gg * SG + SG], cpk[s, 1, :, :], -1.0, None, mul))
            settle()
            dve.sem_inc(s5_c, 1)
            do(V.tensor_tensor(rho[:, :], mag, mag, mul))
            do(V.tensor_tensor(rho[:, :], rho[:, :], rho[:, :], mul))
            do(V.tensor_tensor(rho[:, :], rho[:, :], rho[:, :], mul))
            t16 = [t1[:, 0:NPAIR], t2[:, 0:NPAIR]]
            cur = [cos, sin]
            for k in range(3 + 6):
                nxt = ([sm[9], sm[10]] if k % 2 == 0 else [sm[7], sm[8]]) if k < 2 else [rotF[:, ri, k - 2, :] for ri in range(2)]
                cmul(nxt, cur, cur, t16)
                cur = nxt

            t512 = [tt[:, :].rearrange("p (a b c) -> p a b c", a=RP, b=8) for tt in (t1, t2)]
            for r in range(4):
                pr = slice(RP * r, RP * r + RP)
                n0 = FIRST["s5"] + 10 * r
                cmul([Xp[:, ri, :, 0:P].rearrange("p a (b c) -> p a b c", b=8) for ri in range(2)],
                     [pwR[:, ri, pr, :].unsqueeze(3).to_broadcast([P, RP, 8, SG]) for ri in range(2)],
                     [Bb[:, ri, pr, :].unsqueeze(2).to_broadcast([P, RP, 8, SG]) for ri in range(2)], t512)
                dve.sem_inc(s5_x, 1)
                ap = [pwF[:, ri, pr, 1:9].unsqueeze(3).to_broadcast([P, RP, 8, SG]) for ri in range(2)]
                cc = [cpk[:, ri, pr, :].unsqueeze(2).to_broadcast([P, RP, 8, SG]) for ri in range(2)]
                cav = [ca[:, ri, :, :].rearrange("p a (g b c) -> p a g b c", g=2, b=8) for ri in range(2)]
                mark(V.tensor_tensor(t512[0], ap[0], cc[0], mul))
                mark(V.tensor_tensor(t512[1], ap[1], cc[1], mul))
                settle()
                for gg in range(2):
                    s = slice(64 * gg, 64 * gg + 64)
                    mark(V.tensor_tensor(cav[0][s, :, gg, :, :], t512[0][s], t512[1][s], sub))
                settle()
                mark(V.tensor_tensor(t512[0], ap[0], cc[1], mul))
                mark(V.tensor_tensor(t512[1], ap[1], cc[0], mul))
                settle()
                do(V.tensor_scalar(t1[:, :], t1[:, :], -1.0, None, mul))
                for gg in range(2):
                    s = slice(64 * gg, 64 * gg + 64)
                    mark(V.tensor_tensor(cav[1][s, :, gg, :, :], t512[0][s], t512[1][s], sub))
                settle()
                dve.sem_inc(s5_ca, 1)
                mark(V.memset(E[:, 0, :, 0:1], 1.0))
                mark(V.memset(E[:, 1, :, 0:1], 0.0))
                mark(V.tensor_copy(E[:, :, :, 1], rotF[:, :, 0, pr]))
                settle()
                for k in range(1, 7):
                    w = 1 << k
                    cmul([E[:, ri, :, w:2 * w] for ri in range(2)], [E[:, ri, :, 0:w] for ri in range(2)],
                         [rotF[:, ri, k, pr].unsqueeze(2).to_broadcast([P, RP, w]) for ri in range(2)],
                         [tt[:, 0:RP * w].rearrange("p (a b) -> p a b", a=RP) for tt in (t1, t2)])
                for e in range(2):
                    n = n0 + 6 + e
                    wait_full(dve, n)
                    q = slice(2 * e, 2 * e + 2)
                    w = [banks[n % 8][:, :].rearrange("p (a ri c) -> p ri a c", a=2, ri=2)[:, ri] for ri in range(2)]
                    t = [tt[:, 0:256].rearrange("p (a b) -> p a b", a=2) for tt in (t1, t2)]
                    mark(V.tensor_tensor(t[0], w[0], E[:, 0, q, :], mul))
                    mark(V.tensor_tensor(t[1], w[1], E[:, 1, q, :], mul))
                    settle()
                    do(V.tensor_tensor(v5[:, 0, q, :], t[0], t[1], add))
                    mark(V.tensor_tensor(t[0], w[1], E[:, 0, q, :], mul))
                    mark(V.tensor_tensor(t[1], w[0], E[:, 1, q, :], mul))
                    settle()
                    do(V.tensor_tensor(v5[:, 1, q, :], t[0], t[1], sub))
                    dve.sem_inc(bank_free[n % 8], 1)
                for ri in range(2):
                    for q in range(RP):
                        mark(V.tensor_tensor_scan(z5[:, ri, q, :], rho[:, RP * r + q:RP * r + q + 1].to_broadcast([P, NC8]),
                                                  v5[:, ri, q, :], 0.0, mul, add))
                settle()
                c127 = NC8 - 1
                cmul([xs[:, ri, :, 1:NC8] for ri in range(2)], [E[:, ri, :, 0:c127] for ri in range(2)],
                     [z5[:, ri, :, 0:c127] for ri in range(2)],
                     [tt[:, 0:RP * c127].rearrange("p (a b) -> p a b", a=RP) for tt in (t1, t2)])
                dve.sem_inc(s5_xs, 1)
                dve.wait_ge(s5_du, r + 1)
                for e in range(2):
                    n = n0 + 8 + e
                    dst = uc[:, 8 * r + 4 * e:8 * r + 4 * e + 4, :, :].rearrange("p g i o -> p (g i o)")
                    wait_full(dve, n)
                    V.tensor_tensor(dst, banks[n % 8][:, :], dst, add).then_inc(bank_free[n % 8], 1)
            for e in range(8):
                n = FIRST["yg"] + e
                sl = [y[:, e // 2, :].rearrange("p (c i) -> p i c", i=STEP)[:, 4 * (e % 2):4 * (e % 2) + 4, :] for y in (yhi, ylo)]
                dve.wait_ge(split_hi, 20 + e + 1)
                V.tensor_tensor(sl[1], banks[n % 8][:, :].rearrange("p (i c) -> p i c", i=4), sl[0].bitcast(f32), sub).then_inc(bank_free[n % 8], 1)
            for s in range(2):
                prep_lo(dve, U_GLU + s + 1)
                for j in range(4):
                    n = FIRST["glu"] + 8 * s + 2 * j
                    wait_full(dve, n)
                    wait_taken(dve, n + 1)
                    dve.wait_ge(y_sent[sent % 4], 16 * (sent // 4))
                    V.tensor_tensor(yst[:, sent % 4, :], banks[n % 8][:, :], scr[:, j % 2, :], mul).then_inc(bank_free[n % 8], 1)
                    sent += 1
            tokq = tok[:, :].rearrange("p (i t) -> p i t", i=4)
            dve.wait_ge(acc_zero, 1)
            for counter in (merge_mul, merged, y_lo):
                dve.sem_inc(counter, 1)
            with dve.Fori(0, 3) as b:
                for pc in range(8):
                    half, k = pc // 4, pc % 4
                    h = slice(half * 512, half * 512 + 512)
                    dve.wait_ge(y_hi, b * 8 + pc + 1)
                    V.tensor_tensor(ylo[:, k, h], yst[:, k, :], yhi[:, k, h].bitcast(f32), sub).then_inc(y_lo, 1)
                for s in range(6):
                    prep_lo(dve, U_MERGE + s + 1, b, 6)
                    if s % 3 == 0:
                        continue
                    n0 = FIRST["merge"] + (0, 8, 12, 16, 24, 28)[s]
                    for j in range(4):
                        loc = ((s // 3) * 2 + s % 3 - 1) * 4 + j
                        dd = 2 * ((s // 3) * 2 + s % 3 - 1) + j // 2
                        h = slice((j % 2) * 512, (j % 2) * 512 + 512)
                        tq = tokq[:, dd % 4, h]
                        wait_taken(dve, n0 + j, b, 32)
                        V.tensor_tensor(tq, tq, scr[:, j % 2, :], mul).then_inc(merge_mul, 1)
                        dve.wait_ge(merge_mul, b * 16 + loc + 2)
                        V.tensor_tensor(acc[:, dd, h], acc[:, dd, h], tq, add).then_inc(merged, 1)
            for k in range(KT):
                dve.wait_ge(m_hi, k + 1)
                V.tensor_tensor(hTlo[:, k, :], acc[:, k, :], hThi[:, k, :].bitcast(f32), sub).then_inc(m_lo, 1)
            for s in range(4):
                prep_lo(dve, U_OUT + s + 1)
            yx = yst[:, :, :].rearrange("p (s a) c -> p s (a c)", s=2)

            def residual(t):
                dve.wait_ge(sq_o, t + 1)
                rstd(sumsq[:, 10 + t:11 + t])
                do(V.scalar_tensor_tensor(out=acc[:, t, :], in0=acc[:, t, :], scalar=stat[:, 1:2], in1=tok[:, 0:D], op0=mul, op1=mul))
                dve.wait_ge(x_back[t % 2], 16 * (t // 2 + 1))
                V.tensor_tensor(yx[:, t % 2, :], yx[:, t % 2, :], acc[:, t, :], add).then_inc(x1_made, 1)

            def h2(t):
                dve.wait_ge(sq_x, t + 1)
                rstd(sumsq[:, 18 + t:19 + t])
                V.scalar_tensor_tensor(out=tok[:, (2 + t % 2) * D:(3 + t % 2) * D], in0=yx[:, t % 2, :], scalar=stat[:, 1:2],
                                       in1=tok[:, D:2 * D], op0=mul, op1=mul).then_inc(h2_made, 1)

            def h2_lo(t):
                for e in range(2):
                    n = FIRST["h2"] + 2 * t + e
                    sl = (slice(None), slice(4 * e, 4 * e + 4), slice(t * P, (t + 1) * P))
                    dve.wait_ge(split_hi, 28 + 2 * t + e + 1)
                    V.tensor_tensor(hTlo[sl], banks[n % 8][:, :].rearrange("p (k t) -> p k t", k=4), hThi[sl].bitcast(f32), sub)\
                        .then_inc(bank_free[n % 8], 1)

            dve.wait_ge(post_gains, 32)
            residual(0)
            for t in range(NT):
                if t + 1 < NT:
                    residual(t + 1)
                h2(t)
                if t:
                    h2_lo(t - 1)
            h2_lo(NT - 1)
            dve.wait_ge(acc_zero, 2)

            def mlp(it, last):
                for s in range(2):
                    prep_lo(dve, U_MLP + s + 1, it, 4)
                    for j in range(4):
                        n, pc = FIRST["mlp"] + 4 * s + j, 4 * s + j
                        h = slice((j % 2) * 512, (j % 2) * 512 + 512)
                        wait_taken(dve, n, it, 24)
                        V.tensor_tensor(yst[:, pc % 4, :], scr[:, pc % 2, :], scr[:, pc % 2, :], mul).then_inc(f_sq, 1)
                        dve.wait_ge(f_hi, it * 8 + pc + 1)
                        V.tensor_tensor(ylo[:, 2 * s + j // 2, h], yst[:, pc % 4, :], yhi[:, 2 * s + j // 2, h].bitcast(f32), sub)\
                            .then_inc(f_lo, 1)
                for s in range(2):
                    if not (last and s == 1):
                        prep_lo(dve, U_MLP + 2 + s + 1, it, 4)
                    for t in range(NT):
                        n = FIRST["mlp"] + 8 + 8 * s + t
                        h = slice(s * 512, s * 512 + 512)
                        wait_full(dve, n, it, 24)
                        ins = V.tensor_tensor(acc[:, t, h], banks[n % 8][:, :], acc[:, t, h], add).then_inc(bank_free[n % 8], 1)
                        if last and s == 1:
                            wait_taken(dve, n, it, 24)
                            dve.sem_inc(acc_done, 1)

            with dve.Fori(0, 7) as it:
                mlp(it, False)
            mlp(7, True)
            dve.wait_ge(last_gain, 16)
            for t in range(NT):
                xt = tok[:, (1 + t % 3) * D:(2 + t % 3) * D]
                dve.wait_ge(sq_o, NT + t + 1)
                rstd(sumsq[:, 26 + t:27 + t])
                do(V.scalar_tensor_tensor(out=acc[:, t, :], in0=acc[:, t, :], scalar=stat[:, 1:2], in1=tok[:, 0:D], op0=mul, op1=mul))
                dve.wait_ge(x1_back[t % 3], 16 * (t // 3 + 1))
                V.tensor_tensor(xt, xt, acc[:, t, :], add).then_inc(out_made, 1)

        @block.tensor
        def _(pe):
            T = nc.tensor

            def product(dst, lhs, rhs, kt, start=True, stop=True, ready=None):
                for k in range(kt):
                    if ready:
                        ready(k)
                    for i, (p, q) in enumerate(((0, 0), (0, 1), (1, 0))):
                        ins = T.matmul(dst, lhs(k)[p], rhs(k)[q], start=start and k == 0 and i == 0,
                                       stop=stop and k == kt - 1 and i == 2)
                return ins

            def unit(u, it=0, per=0):
                pe.wait_ge(w_lo, u + 1 + it * per)

            def norm_event(idx, e):
                return FIRST["front"] + (2 * idx + e if idx < 2 else 6 + 6 * ((idx - 2) // 2) + 2 * ((idx - 2) % 2) + e)

            def transposes(n, srcs, dsts=None):
                wait_free(pe, n)
                for i, src in enumerate(srcs):
                    ins = T.transpose(banks[n % 8][:, i * P:i * P + P] if dsts is None else dsts[i], src, ident[:, :])
                ins.then_inc(bank_full[n % 8], 1)

            def norm_transposes(idx):
                pe.wait_ge(h_made, idx + 1)
                for e in range(2):
                    transposes(norm_event(idx, e), [hst[:, idx % 2, (4 * e + i) * P:(4 * e + i + 1) * P] for i in range(4)])

            hT = lambda sl: (lambda k: (hThi[:, k, sl], hTlo[:, k, sl]))
            half = lambda h: slice(h * 512, h * 512 + 512)

            pe.wait_ge(consts, 6)
            norm_transposes(0)
            norm_transposes(1)
            for idx in range(2):
                for e in range(2):
                    wait_taken(pe, norm_event(idx, e))
            for s in range(4):
                n0 = FIRST["front"] + 4 + 6 * s
                unit(s)
                hi, lo = wviews(s, KT)
                for i in range(2):
                    n = n0 + i
                    c = slice(i * P, i * P + P)
                    wait_free(pe, n)
                    if s < 2:
                        ins = product(banks[n % 8][:, 0:256], lambda k: (hi[:, k, c], lo[:, k, c]),
                                      lambda k: (mThi[:, k, :], mTlo[:, k, :]), KT)
                    else:
                        ins = product(banks[n % 8][:, 0:256], lambda k: (mThi[:, k, c], mTlo[:, k, c]),
                                      lambda k: (hi[:, k, :], lo[:, k, :]), KT)
                    ins.then_inc(bank_full[n % 8], 1)
                norm_transposes(2 + 2 * s)
                norm_transposes(3 + 2 * s)

            def project(u, n0):
                unit(u)
                w = [v.rearrange("p k (i c) -> p k i c", i=2) for v in wviews(u, KT)]
                for j in range(4):
                    n = n0 + j
                    wait_free(pe, n)
                    product(banks[n % 8][:, :], lambda k: (w[0][:, k, j // 2], w[1][:, k, j // 2]), hT(half(j % 2)), KT)\
                        .then_inc(bank_full[n % 8], 1)

            for idx in range(2, 10):
                for e in range(2):
                    wait_taken(pe, norm_event(idx, e))
            for s in range(2):
                project(U_QX + s, FIRST["qx"] + 4 * s)
            tokq = tok[:, :].rearrange("p (i t) -> p i t", i=4)
            for n in range(FIRST["qx"], FIRST["qx"] + 8):
                wait_taken(pe, n)
            for e in range(16):
                n = FIRST["xsc"] + e
                wait_free(pe, n)
                for hh in range(2):
                    h = 2 * (e % 2) + hh
                    ins = T.matmul(banks[n % 8][:, hh * 256:hh * 256 + 256], tokq[:, h, (e // 2) * P:(e // 2 + 1) * P],
                                   kmT[:, h, :], start=True, stop=True)
                ins.then_inc(bank_full[n % 8], 1)
            for s in range(2):
                project(U_Q + s, FIRST["q"] + 4 * s)
            project(U_KV, FIRST["kv"])
            pe.wait_ge(x_prob, 16)

            def x_transposes(q):
                h, hf = q // 2, q % 2
                for m in range(2):
                    c = (h % 2) * 256 + m * P
                    transposes(FIRST["xpv"] + pv_event(q, m), [prob[:, 2 * (4 * hf + t) + h // 2, c:c + P] for t in range(4)])

            x_transposes(0)
            for q in range(8):
                if q < 7:
                    x_transposes(q + 1)
                n = FIRST["xpv"] + pv_event(q, 2)
                for m in range(2):
                    wait_taken(pe, FIRST["xpv"] + pv_event(q, m))
                wait_free(pe, n)
                h = q // 2
                for m in range(2):
                    ins = T.matmul(banks[n % 8][:, :], vm[:, m, h * P:h * P + P], pT[:, q % 2, m, :], start=m == 0, stop=m == 1)
                ins.then_inc(bank_full[n % 8], 1)
            for e in range(10):
                n = FIRST["rope"] + e
                src = qwin[:, e // 4, (e // 2) % 2, 8 * (e % 2):8 * (e % 2) + 8, :] if e < 8 else kT[:, half(e % 2)]
                wait_taken(pe, FIRST["q"] + e)
                wait_free(pe, n)
                T.matmul(banks[n % 8][:, :], rotm[:, :], src, start=True, stop=True).then_inc(bank_full[n % 8], 1)
            for n in (FIRST["kv"] + 2, FIRST["kv"] + 3):
                wait_taken(pe, n)
            for e in range(4):
                starts = [max(0, 64 * (4 * e + i - 1)) for i in range(4)]
                transposes(FIRST["vwin"] + e, [vT[:, s0:s0 + P] for s0 in starts])
            pe.wait_ge(rope_done, 10)
            for e in range(16):
                n = FIRST["ssc"] + e
                j = e % 2
                rows = slice(64 * j, 64 * j + 64)
                wait_free(pe, n)
                for sl in range(4):
                    ch, pair = 2 * (e // 2) + sl // 2, sl % 2
                    k0, nk = (0, 64) if ch == 0 else (64 * (ch - 1), P)
                    ins = T.matmul(banks[n % 8][:, sl * P:sl * P + nk], qflat[rows, pair, ch, :],
                                   kT[rows, k0:k0 + nk], start=True, stop=True)
                ins.then_inc(bank_full[n % 8], 1)
            hs = [h[:, :, :].rearrange("p k (c i) -> p k i c", i=STEP) for h in (hThi, hTlo)]
            for s in range(2):
                u = U_U + s
                unit(u)
                hi, lo = wviews(u, KT)
                for jj in range(4):
                    n = FIRST["u"] + 4 * s + jj
                    wait_free(pe, n)
                    for ii in range(2):
                        i = 2 * jj + ii
                        ins = product(banks[n % 8][:, ii * 256:ii * 256 + 256], lambda k: (hs[0][:, k, i, :], hs[1][:, k, i, :]),
                                      lambda k: (hi[:, k, :], lo[:, k, :]), KT)
                    ins.then_inc(bank_full[n % 8], 1)
            pe.wait_ge(s_prob, 16)
            for e in range(4):
                wait_taken(pe, FIRST["vwin"] + e)

            def s_transposes(q):
                for nn in range(2):
                    n = FIRST["spv"] + pv_event(q, nn)
                    nk = 64 if q == 0 and nn == 0 else P
                    transposes(n, [prob[:, 2 * q + ja // 2, (2 * nn + ja % 2) * P:(2 * nn + ja % 2) * P + nk] for ja in range(4)],
                               [banks[n % 8][0:nk, ja * P:ja * P + P] for ja in range(4)])

            s_transposes(0)
            for q in range(8):
                if q < 7:
                    s_transposes(q + 1)
                n = FIRST["spv"] + pv_event(q, 2)
                for nn in range(2):
                    wait_taken(pe, FIRST["spv"] + pv_event(q, nn))
                wait_free(pe, n)
                for nn in range(2):
                    nk = 64 if q == 0 and nn == 0 else P
                    for j in range(2):
                        ins = T.matmul(banks[n % 8][64 * j:64 * j + 64, nn * 256:nn * 256 + 256],
                                       vwin[0:nk, 2 * q + nn, 64 * j:64 * j + 64], pT[0:nk, q % 2, nn, j * 256:j * 256 + 256],
                                       start=True, stop=True)
                ins.then_inc(bank_full[n % 8], 1)
            pe.wait_ge(s5_dt, 1)
            n = FIRST["spar"]
            wait_free(pe, n)
            for k in range(3):
                ins = T.transpose(banks[n % 8][:, 16 * k:16 * k + 16], sload[:, k, :], ident[0:NPAIR, 0:NPAIR])
            ins.then_inc(bank_full[n % 8], 1)
            for ri in range(2):
                transposes(FIRST["spar"] + 1 + ri, [craw[:, ri, r, :, :].rearrange("p d x -> p (d x)") for r in range(4)])
            for n in range(FIRST["u"], FIRST["u"] + 8):
                wait_taken(pe, n)
            for r in range(4):
                n0 = FIRST["s5"] + 10 * r
                for e in range(2):
                    transposes(n0 + e, [uc[:, 8 * r + g, :, :].rearrange("p i c -> p (i c)") for g in range(4 * e, 4 * e + 4)])
                pe.wait_ge(s5_x, r + 1)
                for ri in range(2):
                    transposes(n0 + 2 + ri, [Xp[:, ri, q, 0:P] for q in range(RP)])
                if r == 0:
                    pe.wait_ge(s5_c, 1)
                for e in range(2):
                    n = n0 + 4 + e
                    wait_free(pe, n)
                    for q in range(2):
                        for i in range(STEP):
                            for ri in range(2):
                                ins = T.matmul(banks[n % 8][:, q * 256 + i * 32:q * 256 + i * 32 + 32],
                                               Xp[:, ri, 2 * e + q, (7 - i) * SG:(7 - i) * SG + P],
                                               cbd[:, ri, RP * r + 2 * e + q, :], start=ri == 0, stop=ri == 1)
                    ins.then_inc(bank_full[n % 8], 1)
                for e in range(4):
                    wait_taken(pe, n0 + e)
                for e in range(2):
                    n = n0 + 6 + e
                    wait_free(pe, n)
                    for q in range(2):
                        for ri in range(2):
                            for g in range(2):
                                ins = T.matmul(banks[n % 8][64 * g:64 * g + 64, (2 * q + ri) * P:(2 * q + ri) * P + P],
                                               wT[:, ri, 2 * e + q, 64 * g:64 * g + 64], uT[:, 2 * (2 * e + q) + g, :],
                                               start=True, stop=True)
                    ins.then_inc(bank_full[n % 8], 1)
                for e in range(2):
                    wait_taken(pe, n0 + 4 + e)
                pe.wait_ge(s5_ca, r + 1)
                pe.wait_ge(s5_xs, r + 1)
                for e in range(2):
                    n = n0 + 8 + e
                    wait_free(pe, n)
                    for q in range(2):
                        pr = 2 * e + q
                        for ri in range(2):
                            T.matmul(banks[n % 8][:, q * 256:q * 256 + 256], xs[:, ri, pr, :], ca[:, ri, pr, :],
                                     start=ri == 0, stop=False, skip_group_check=True)
                        for g in range(2):
                            ins = T.matmul(banks[n % 8][:, q * 256 + g * P:q * 256 + g * P + P], uT[:, 2 * pr + g, :], Mt[:, 2 * pr + g, :],
                                           start=False, stop=g == 1, skip_group_check=True)
                    ins.then_inc(bank_full[n % 8], 1)
            for e in range(8):
                pe.wait_ge(gelu_done, e // 2 + 1)
                transposes(FIRST["yg"] + e, [gl[e // 2][:, 4 * (e % 2) + i, :] for i in range(4)])
            for e in range(8):
                wait_taken(pe, FIRST["yg"] + e)
            yT = lambda sl: (lambda k: (yhi[:, k, sl], ylo[:, k, sl]))
            for s in range(2):
                u = U_GLU + s
                unit(u)
                hi, lo = wviews(u, BT)
                for j in range(4):
                    for ag in range(2):
                        n = FIRST["glu"] + 8 * s + 2 * j + ag
                        c = slice(ag * 256 + (j // 2) * P, ag * 256 + (j // 2) * P + P)
                        wait_free(pe, n)
                        product(banks[n % 8][:, :], lambda k: (hi[:, k, c], lo[:, k, c]), yT(half(j % 2)), BT).then_inc(bank_full[n % 8], 1)
            with pe.Fori(0, 3) as b:
                for s in range(6):
                    n0 = FIRST["merge"] + (0, 8, 12, 16, 24, 28)[s]
                    u = U_MERGE + s
                    unit(u, b, 6)
                    kt = BT if s % 3 == 0 else KT
                    hi, lo = wviews(u, kt)
                    for j in range(8 if s % 3 == 0 else 4):
                        n = n0 + j
                        c = slice((j // 2) * P, (j // 2) * P + P)
                        wait_free(pe, n, b, 32)
                        if s == 0 and j < 2:
                            pe.wait_ge(y_lo, b * 8 + 4 * (j + 1) + 1)
                        product(banks[n % 8][:, :], lambda k: (hi[:, k, c], lo[:, k, c]),
                                (yT if s % 3 == 0 else hT)(half(j % 2)), kt).then_inc(bank_full[n % 8], 1)
            for s in range(4):
                u = U_OUT + s
                unit(u)
                hi, lo = wviews(u, KT)
                for j in range(4):
                    n = FIRST["wout"] + 4 * s + j
                    wait_free(pe, n)
                    for tt in range(2):
                        t = 2 * j + tt
                        ready = (lambda k: pe.wait_ge(m_lo, k + 1)) if s == 0 and t == 0 else None
                        ins = product(banks[n % 8][:, tt * 256:tt * 256 + 256], hT(slice(t * P, t * P + P)),
                                      lambda k: (hi[:, k, :], lo[:, k, :]), KT, ready=ready)
                    ins.then_inc(bank_full[n % 8], 1)
            for t in range(NT):
                pe.wait_ge(h2_made, t + 1)
                for e in range(2):
                    c = (2 + t % 2) * D + 4 * e * P
                    transposes(FIRST["h2"] + 2 * t + e, [tok[:, c + i * P:c + i * P + P] for i in range(4)])
            for n in range(FIRST["h2"] + 8, FIRST["h2"] + 16):
                wait_taken(pe, n)

            def mlp(it):
                for s in range(2):
                    u = U_MLP + s
                    unit(u, it, 4)
                    hi, lo = wviews(u, KT)
                    for j in range(4):
                        n = FIRST["mlp"] + 4 * s + j
                        c = slice((j // 2) * P, (j // 2) * P + P)
                        wait_free(pe, n, it, 24)
                        product(banks[n % 8][:, :], lambda k: (hi[:, k, c], lo[:, k, c]), hT(half(j % 2)), KT).then_inc(bank_full[n % 8], 1)
                for s in range(2):
                    u = U_MLP + 2 + s
                    unit(u, it, 4)
                    hi, lo = wviews(u, BT)
                    for t in range(NT):
                        n = FIRST["mlp"] + 8 + 8 * s + t
                        wait_free(pe, n, it, 24)
                        if s == 0 and t in (0, 4):
                            pe.wait_ge(f_lo, it * 8 + (7 if t == 0 else 8))
                        product(banks[n % 8][:, :], yT(slice(t * P, t * P + P)), lambda k: (hi[:, k, :], lo[:, k, :]), BT)\
                            .then_inc(bank_full[n % 8], 1)

            with pe.Fori(0, 8) as it:
                mlp(it)


_INS = ["x", "mem", "positions", "g_mix_pre", "g_mix_post", "g_mem", "g_mlp_pre", "g_mlp_post", "sinks", "w_in", "w_mem_kv",
        "ssm_A_re", "ssm_A_im", "ssm_log_dt", "ssm_B_re", "ssm_B_im", "ssm_C_re", "ssm_C_im", "ssm_D", "w_glu",
        "w_branch_attn", "w_branch_ssm", "w_branch_mem", "w_out", "w_up", "w_down"]


def kernel(**inputs):
    import numpy as _np
    import concourse.bacc as _bacc
    from concourse import mybir as _mybir
    from concourse.bass_utils import run_bass_kernel_spmd as _run

    nc = _bacc.Bacc("TRN2", target_bir_lowering=False, num_devices=1)
    arrays, args = {}, {}
    for name in _INS:
        arrays[name] = _np.ascontiguousarray(inputs[name])
    freq = (10000.0 ** (-_np.arange(HD // 2, dtype=_np.float64) / (HD // 2))).astype(_np.float32)
    arrays["inv_freq"] = _np.tile(freq, P // (HD // 2)).reshape(P, 1)
    feed = {}
    for name, arr in arrays.items():
        feed[f"in_{name}_dram"] = arr
        args[name] = nc.dram_tensor(f"in_{name}_dram", arr.shape, _mybir.dt.from_np(arr.dtype), kind="ExternalInput").ap()
    out = nc.dram_tensor("out_0_dram", (1, L, D), _mybir.dt.float32, kind="ExternalOutput").ap()
    hybrid_layer(nc, args, out)
    r = _run(nc, [feed], core_ids=[0])
    return r.results[0]["out_0_dram"]
```

```python
from contextlib import ExitStack, contextmanager

import numpy as np
import concourse.bass as bass
from concourse import mybir

P = 128
D = 1024
L = 1024
KT = D // P
NT = L // P
MEM = 256
HD = 64
CH = 64
NCH = L // CH
W512 = 512
BT = W512 // P
XH = 4
DFF = 4096
EPS = 1e-6
STEP = 8
NC8 = L // STEP
NPAIR = 16
SG = 16
ST = 64
RP = 4
C_V, C_U, C_QX, C_G = 640, 768, 1280, 1792
UNIT = 2048

U_MEM, U_QX, U_Q, U_KV, U_U, U_MERGE_A, U_GLU, U_MERGE_M, U_MERGE_S, U_OUT, U_MLP = 0, 4, 6, 8, 10, 23, 25, 27, 29, 31, 35
U_GATE = [9, 12, 13] + list(range(14, 23))
STAGES = [("front", 28), ("spar", 1), ("qx", 8), ("xsc", 16), ("q", 8), ("kv", 4), ("xpv", 24), ("rope", 10), ("vwin", 4),
          ("g0", 4), ("ssc", 16), ("u", 8), ("g1", 4), ("spv", 24), ("g2", 4), ("spc", 2), ("s5a0", 6), ("g3", 4),
          ("s5m0", 2), ("g4", 4), ("s5y0", 2), ("s5a1", 6), ("g5", 4), ("s5m1", 2), ("g6", 4), ("s5y1", 2), ("s5a2", 6),
          ("g7", 4), ("s5m2", 2), ("g8", 4), ("s5y2", 2), ("s5a3", 6), ("g9", 4), ("s5m3", 2), ("g10", 4), ("s5y3", 2), ("g11", 4), ("yg", 8), ("mergeA", 16),
          ("glu", 16), ("mergeM", 16), ("mergeS", 16), ("out", 32), ("mlp", 192)]
OUT_ORDER = ["w0", "w1", "w2", "h0", "w3", "h1", "w4", "h2", "w5", "h3", "w6", "h4", "w7", "h5", "h6", "h7"]
FIRST = {}
_n = 0
for _name, _count in STAGES:
    FIRST[_name] = _n
    _n += _count

RSQRT_SEED = float(0x5F3759DF)
MAGIC = 12582912.0


def _chunks_of(value, bits, n):
    out = []
    for _ in range(n - 1):
        e = int(np.floor(np.log2(abs(value))))
        c = float(np.floor(value / 2.0 ** (e - bits + 1)) * 2.0 ** (e - bits + 1))
        out.append(c)
        value -= c
    return out + [float(np.float32(value))]


TWO_PI = _chunks_of(2 * np.pi, 8, 4)
LN2 = _chunks_of(np.log(2.0), 12, 2)
PI_DOWN = float(np.float32(3.1415925))


def pv_event(g, part):
    if part < 2:
        return part if g == 0 else 2 + 3 * (g - 1) + part
    return 4 + 3 * g if g < 7 else 23


LAST_DOWN = [(0, 0), (1, 0), (0, 1), (1, 1)] + [(t, s) for t in range(2, 8) for s in range(2)]


def gate_piece(gp):
    return gp // 16, gp % 16 // 2, gp % 2


def out_event(kind, t, e):
    return FIRST["out"] + 2 * OUT_ORDER.index(f"{kind}{t}") + e


def hybrid_layer(nc, a, out):
    f32, f32r, i32 = mybir.dt.float32, mybir.dt.float32r, mybir.dt.int32
    ALU, ACT, AX = mybir.AluOpType, mybir.ActivationFunctionType, mybir.AxisListType
    add, sub, mul = ALU.add, ALU.subtract, ALU.mult
    ctx = ExitStack()
    with ctx:
        def sb(name, shape, dt=f32, stack=ctx):
            return stack.enter_context(nc.sbuf_tensor(name, shape, dt))

        def sem(name):
            return ctx.enter_context(nc.semaphore(name))

        @contextmanager
        def overlay():
            with ExitStack() as stack:
                yield lambda name, shape, dt=f32: sb(name, shape, dt, stack)

        ident = sb("ident", [P, P])
        rotm = sb("rotm", [P, P])
        halfpi = sb("halfpi", [P, 1])
        stat = sb("stat", [P, 8])
        rs = sb("rs", [P, 10])
        sumsq = sb("sumsq", [P, 40])
        mx = sb("mx", [P, 64])
        den = sb("den", [P, 64])
        sinkb = sb("sinkb", [P, 4])
        smalli = sb("smalli", [P, NPAIR], i32)
        sinkx = sb("sinkx", [P, 16, 4])
        ldt = sb("ldt", [NPAIR, 2])
        raw = sb("raw", [P, 2, UNIT])
        whi = sb("whi", [P, 2, UNIT], f32r)
        wlo = sb("wlo", [P, 2, UNIT], f32r)
        hThi = sb("hThi", [P, KT, L], f32r)
        hTlo = sb("hTlo", [P, KT, L], f32r)
        tok = sb("tok", [P, 4096])
        rho = sb("rho", [P, NPAIR])
        yst = sb("yst", [P, 4, 512])
        yst2 = yst[:, 0:2, :]
        second = yst[:, 2:4, :].rearrange("p a b -> p (a b)")
        cut = lambda lo, n: second[:, lo:lo + n]
        spar = cut(0, 48).rearrange("p (a k) -> p a k", a=3)
        pwF = cut(48, 288).rearrange("p (a k b) -> p a k b", a=2, b=9)
        pwR = cut(336, 256).rearrange("p (a k b) -> p a k b", a=2, b=8)
        rotF = cut(592, 224).rearrange("p (a b k) -> p a b k", a=2, b=7)
        small = cut(816, 192).rearrange("p (a k) -> p a k", a=12)
        scr = sb("scr", [P, 2, 512])
        with ExitStack() as att:
            kmT = sb("kmT", [P, XH, MEM], f32, att)
            vm = sb("vm", [P, 2, W512], f32, att)
            kT = sb("kT", [P, L], f32, att)
            vT = sb("vT", [P, L], f32, att)
            with overlay() as ov:
                mThi = ov("mThi", [P, KT, MEM], f32r)
                mTlo = ov("mTlo", [P, KT, MEM], f32r)
                xst = ov("xst", [P, 3, D])
                hst = ov("hst", [P, 2, D])
                gpre = ov("gpre", [P, D])
                gmem = ov("gmem", [P, D])
                junk = ov("junk", [P, D])
            with overlay() as ov:
                prob = ov("prob", [P, 16, 512])
                pT = ov("pT", [P, 2, 2, 512])
                with overlay() as ov2:
                    cosT = ov2("cosT", [P, L])
                    sinT = ov2("sinT", [P, L])
                with overlay() as ov2:
                    vwin = ov2("vwin", [P, NCH, P])
        with overlay() as ov:
            sB = ov("sB", [P, 2, NPAIR, SG])
            Bb = ov("Bb", [P, 2, NPAIR, SG])
            cpk = ov("cpk", [P, 2, NPAIR, SG])
            Dbc = ov("Dbc", [P, W512])
            Xp = ov("Xp", [P, 2, RP, P])
            near = ov("near", [P, 2, 2, RP, P])
            ca = ov("ca", [P, 2, RP, 2 * 9 * SG])
            Mt = ov("Mt", [P, 2 * RP, P])
            wT = ov("wT", [P, 2, RP, P])
            uT = ov("uT", [P, 2 * RP, P])
            E = ov("E", [P, 2, RP, NC8])
            v5 = ov("v5", [P, 2, RP, NC8])
            z5 = ov("z5", [P, 2, RP, NC8])
            xs = ov("xs", [P, 2, RP, NC8])
            t1 = ov("t1", [P, 512])
            t2 = ov("t2", [P, 512])
            t3 = ov("t3", [P, 512])
            t4 = ov("t4", [P, 512])
        with overlay() as ov:
            yhi = ov("yhi", [P, BT, L], f32r)
            ylo = ov("ylo", [P, BT, L], f32r)
            acc = ov("acc", [P, KT, L])
        xtile = lambda idx: xst[:, idx % 7, :] if idx % 7 < 3 else tok[:, (idx % 7 - 3) * D:(idx % 7 - 2) * D]
        qwin = tok[:, :].rearrange("p (a n h c) -> p a h n c", a=2, n=NCH, h=2)
        qflat = tok[:, :].rearrange("p (a n x) -> p a n x", a=2, n=NCH)
        uc = tok[:, :].rearrange("p (g i c) -> p g i c", g=32, i=STEP)
        gl = [t[:, :, :, :].rearrange("p a b c -> p (a b) c") for t in (E, v5, z5, xs)]
        craw = z5[:, :, :, :].rearrange("p a r (d x) -> p a r d x", d=2)
        sload = scr[0:NPAIR, 0, 0:384].rearrange("p (a x) -> p a x", a=3)

        y_dram = nc.dram_tensor("y_scratch", (2, BT, P, L), f32, kind="Internal").ap()
        g_dram = nc.dram_tensor("gate_scratch", (3, KT, P, L), f32, kind="Internal").ap()
        x1_dram = nc.dram_tensor("x1_scratch", (L, D), f32, kind="Internal").ap()

        banks = [ctx.enter_context(nc.psum_tensor(f"bank{b}", [P, 512], f32)) for b in range(8)]
        bank_full = [sem(f"bank_full{b}") for b in range(8)]
        bank_free = [sem(f"bank_free{b}") for b in range(8)]
        w_loaded = [sem(f"w_loaded{s}") for s in range(2)]
        w_hi, w_lo = sem("w_hi"), sem("w_lo")
        consts = sem("consts")
        gains_in, gain2_in = sem("gains_in"), sem("gain2_in")
        pos_in = sem("pos_in")
        sinks_in = sem("sinks_in")
        mem_in = [sem(f"mem_in{s}") for s in range(2)]
        tile_in = [sem(f"tile_in{s}") for s in range(7)]
        square_sum = sem("square_sum")
        h_made = sem("h_made")
        split_hi = sem("split_hi")
        trig_arg, trig_done = sem("trig_arg"), sem("trig_done")
        x_exp, x_prob = sem("x_exp"), sem("x_prob")
        s_exp, s_prob, sink_arg, sink_exp = sem("s_exp"), sem("s_prob"), sem("sink_arg"), sem("sink_exp")
        rope_done = sem("rope_done")
        y_sent = [sem(f"y_sent{s}") for s in range(2)]
        g_sent = [sem(f"g_sent{s}") for s in range(2)]
        gate_in = [sem(f"gate_in{s}") for s in range(4)]
        y_loaded = [sem(f"y_loaded{s}") for s in range(4)]
        y_hi, y_lo = sem("y_hi"), sem("y_lo")
        s5_in, s5_small_in = sem("s5_in"), sem("s5_small_in")
        s5_near, s5_dt = sem("s5_near"), sem("s5_dt")
        s5_trig, s5_trig_done = sem("s5_trig"), sem("s5_trig_done")
        s5_x, s5_ca, s5_xs, s5_du, gelu_done = sem("s5_x"), sem("s5_ca"), sem("s5_xs"), sem("s5_du"), sem("gelu_done")
        acc_zero = sem("acc_zero")
        merged = sem("merged")
        m_hi, m_lo = sem("m_hi"), sem("m_lo")
        post_gains = sem("post_gains")
        x_back, x1_made, x1_sent, h2_made = [sem("x_back0"), sem("x_back1")], sem("x1_made"), sem("x1_sent"), sem("h2_made")
        sq_o, sq_x = sem("sq_o"), sem("sq_x")
        f_sq, f_hi, f_lo = sem("f_sq"), sem("f_hi"), sem("f_lo")
        acc_done = sem("acc_done")
        last_gain = sem("last_gain")
        x1_back = [sem(f"x1_back{s}") for s in range(3)]
        out_made, out_sent = sem("out_made"), [sem(f"out_sent{s}") for s in range(3)]
        chain = sem("chain")
        block = ctx.enter_context(nc.Block())

        def wait_free(eng, n, it=0, per=0):
            if n >= 8:
                eng.wait_ge(bank_free[n % 8], n // 8 + it * (per // 8))

        def wait_full(eng, n, it=0, per=0):
            eng.wait_ge(bank_full[n % 8], n // 8 + 1 + it * (per // 8))

        def wait_taken(eng, n, it=0, per=0):
            eng.wait_ge(bank_free[n % 8], n // 8 + 1 + it * (per // 8))

        def parts(u):
            if u in (U_OUT + 2, U_OUT + 3):
                h = slice(2 * (u - U_OUT - 2), 2 * (u - U_OUT - 2) + 2)
                return [y[:, h, :].rearrange("p a b -> p (a b)") for y in (yhi, ylo)]
            return [w[:, u % 2, :] for w in (whi, wlo)]

        def prep_hi(act, u, n_before, it=0, per=0, ev=0):
            dmas = 2 * (u // 2 + 1) + (2 if u >= U_Q else 0)
            act.wait_ge(w_loaded[u % 2], 16 * dmas + it * (16 * per))
            if n_before is not None:
                wait_full(act, n_before, it, ev)
            nc.scalar.activation(parts(u)[0], raw[:, u % 2, :], ACT.Copy).then_inc(w_hi, 1)

        def prep_lo(dve, u, it=0, per=0):
            hi, lo = parts(u)
            dve.wait_ge(w_hi, u + 1 + it * per)
            nc.vector.tensor_tensor(lo, raw[:, u % 2, :], hi.bitcast(f32), sub).then_inc(w_lo, 1)

        def wviews(u, kt):
            w = UNIT // kt
            return (whi[:, u % 2, :].rearrange("p (k c) -> p k c", c=w), wlo[:, u % 2, :].rearrange("p (k c) -> p k c", c=w))

        @block.sync
        def _(sp):
            def load(u, pieces, it=0, per=0):
                if u >= 2:
                    sp.wait_ge(w_lo, u - 1 + it * per)
                for dst, src in pieces:
                    sp.dma_start(dst, src).then_inc(w_loaded[u % 2], 16)

            def cols(u, src, kt=KT):
                v = raw[:, u % 2, :].rearrange("p (k c) -> p k c", k=kt)
                s = src.rearrange("(k p) c -> p k c", p=P)
                h = kt // 2
                return [(v[:, 0:h, :], s[:, 0:h, :]), (v[:, h:kt, :], s[:, h:kt, :])]

            for idx in range(2):
                sp.dma_start(xst[:, idx, :], a["mem"][0][idx * P:(idx + 1) * P, :]).then_inc(mem_in[idx], 16)
            sp.dma_start(gmem[:, :], a["g_mem"][0].partition_broadcast(P)).then_inc(gains_in, 16)
            w_in = a["w_in"][0]
            for s in range(4):
                load(U_MEM + s, cols(U_MEM + s, a["w_mem_kv"][0][:, s * 256:(s + 1) * 256]))
            for s in range(2):
                load(U_QX + s, cols(U_QX + s, w_in[:, C_QX + s * 256:C_QX + (s + 1) * 256]))
            for s in range(2):
                u = U_Q + s
                v = raw[:, u % 2, :].rearrange("p (k i j c) -> p k i j c", k=KT, i=2, j=2)
                src = w_in[:, 0:512].rearrange("(k p) (j i c) -> p k i j c", p=P, j=2, c=HD)
                load(u, [(v[:, :, i, j, :], src[:, :, 2 * s + i, j, :]) for i in range(2) for j in range(2)])
            load(U_KV, cols(U_KV, w_in[:, 512:768]))
            gate = lambda i: load(U_GATE[i], cols(U_GATE[i], w_in[:, C_G + 256 * i:C_G + 256 * (i + 1)]))
            gate(0)
            for s in range(2):
                load(U_U + s, cols(U_U + s, w_in[:, C_U + s * 256:C_U + (s + 1) * 256]))
            for i in range(1, 12):
                gate(i)
            for s in range(2):
                u = U_MERGE_A + s
                v = raw[:, u % 2, :].rearrange("p (k c) -> p k c", k=BT)
                load(u, [(v[64 * j:64 * j + 64, :, :], a["w_branch_attn"][0][256 * j:256 * j + 256, s * 512:s * 512 + 512]
                          .rearrange("(k p) c -> p k c", p=HD)) for j in range(2)])
            for s in range(2):
                u = U_GLU + s
                v = raw[:, u % 2, :].rearrange("p (k h c) -> p k h c", k=BT, h=2)
                src = a["w_glu"][0].rearrange("(k p) (h c) -> p k h c", p=P, h=2)
                load(u, [(v[:, :, h, :], src[:, :, h, s * 256:(s + 1) * 256]) for h in range(2)])
            for first, name in ((U_MERGE_M, "w_branch_mem"), (U_MERGE_S, "w_branch_ssm")):
                for s in range(2):
                    load(first + s, cols(first + s, a[name][0][:, s * 512:s * 512 + 512], BT))
            for s, c in enumerate((1, 0, 2, 3)):
                load(U_OUT + s, cols(U_OUT + s, a["w_out"][0][:, c * 256:(c + 1) * 256]))
            up, down = a["w_up"][0], a["w_down"][0]
            with sp.Fori(0, 8) as it:
                for s in range(2):
                    load(U_MLP + s, cols(U_MLP + s, up[:, bass.ds(it * 512 + s * 256, 256)]), it, 4)
                for s in range(2):
                    load(U_MLP + 2 + s, cols(U_MLP + 2 + s, down[bass.ds(it * 512, 512), s * 512:(s + 1) * 512], BT), it, 4)
            for t in range(NT):
                sp.wait_ge(out_made, t + 1)
                sp.dma_start(out[0, t * P:(t + 1) * P, :], tok[:, (1 + t % 3) * D:(2 + t % 3) * D]).then_inc(out_sent[t % 3], 16)
            for s, count in enumerate((3, 3, 2)):
                sp.wait_ge(out_sent[s], 16 * count)

        @block.gpsimd
        def _(pool):
            g = nc.gpsimd
            g.memset(ident[:, :], 0.0).then_inc(consts, 1)
            g.memset(rotm[:, :], 0.0).then_inc(consts, 1)
            g.memset(halfpi[:, :], float(np.float32(np.pi / 2))).then_inc(consts, 1)
            pool.wait_ge(consts, 3)
            g.affine_select(out=ident[:, :], in_=ident[:, :], compare_op=ALU.not_equal, fill=1.0, base=0,
                            pattern=[[-1, P]], channel_multiplier=1).then_inc(consts, 1)
            rv = rotm[:, :].rearrange("p (b h c) -> p b h c", b=2, h=2)
            for h, fill, base in ((0, -1.0, -32), (1, 1.0, 0)):
                g.affine_select(out=rv[:, :, h, :], in_=rv[:, :, h, :], compare_op=ALU.not_equal, fill=fill, base=base,
                                pattern=[[-64, 2], [-1, 32]], channel_multiplier=1).then_inc(consts, 1)
            x = a["x"][0]
            for idx in range(2, 10):
                if idx >= 7:
                    pool.wait_ge(h_made, idx - 6)
                g.dma_start(xtile(idx), x[(idx - 2) * P:(idx - 1) * P, :]).then_inc(tile_in[idx % 7], 16)
                if idx == 2:
                    g.dma_start(gpre[:, :], a["g_mix_pre"][0].partition_broadcast(P)).then_inc(gain2_in, 16)
                if idx == 3:
                    for k, name in enumerate(("ssm_A_re", "ssm_A_im")):
                        g.dma_start(sload[:, k, :], a[name][0].rearrange("(k g) p -> k (g p)", g=2)).then_inc(s5_small_in, 16)
                    g.dma_start(ldt[:, :], a["ssm_log_dt"][0].rearrange("(k g) -> k g", g=2)).then_inc(s5_small_in, 16)
            g.dma_start(yst2[:, :, :].rearrange("p a b -> p (a b)").bitcast(i32),
                        a["positions"][0].partition_broadcast(P)).then_inc(pos_in, 16)
            g.dma_start(stat[:, 7:8], a["inv_freq"]).then_inc(pos_in, 16)
            sk = a["sinks"][0].rearrange("(c h) -> h c", h=2)
            for h in range(2):
                g.dma_start(sinkb[64 * h:64 * h + 64, :], sk[h].partition_broadcast(64), allow_slow_non_contiguous=True).then_inc(sinks_in, 16)

            def gates_out(i):
                for gp in range(4 * i, 4 * i + 4):
                    b, d, h = gate_piece(gp)
                    wait_taken(pool, FIRST[f"g{i}"] + gp % 4)
                    g.dma_start(g_dram[b, d, :, h * 512:h * 512 + 512], scr[:, gp % 2, :]).then_inc(g_sent[gp % 2], 16)

            for q in range(8):
                wait_taken(pool, FIRST["xpv"] + pv_event(q, 2))
                g.dma_start(y_dram[1, q // 2, :, (q % 2) * 512:(q % 2) * 512 + 512], yst2[:, q % 2, :]).then_inc(y_sent[q % 2], 16)
            gates_out(0)
            gates_out(1)
            for q in range(8):
                wait_taken(pool, FIRST["spv"] + pv_event(q, 2))
                g.dma_start(y_dram[0, :, :, q * P:(q + 1) * P].rearrange("i p t -> p i t"),
                            yst2[:, q % 2, :].rearrange("p (i t) -> p i t", i=4)).then_inc(y_sent[q % 2], 16)
            for k, name in enumerate(("ssm_B_re", "ssm_B_im")):
                g.dma_start(sB[:, k, :, :], a[name][0].rearrange("(k g) p c -> (g p) k c", g=2)).then_inc(s5_in, 16)
            for k, name in enumerate(("ssm_C_re", "ssm_C_im")):
                for d in range(2):
                    g.dma_start(craw[:, k, :, d, :], a[name][0].rearrange("(r g) o p -> (g o) r p", r=4)).then_inc(s5_in, 16)
            g.dma_start(Dbc[:, :], a["ssm_D"][0].partition_broadcast(P)).then_inc(s5_in, 16)
            gates_out(2)
            pool.wait_ge(s5_in, 112)
            for r in range(4):
                for e in range(2):
                    wait_taken(pool, FIRST[f"s5a{r}"] + e)
                sl = uc[:, 8 * r:8 * r + 8, :, :]
                dd = Dbc[:, P * r:P * r + P].rearrange("p (g c) -> p g c", c=SG).unsqueeze(2).to_broadcast([P, 8, STEP, SG])
                g.tensor_tensor(sl, sl, dd, mul).then_inc(s5_du, 1)
                pool.wait_ge(s5_x, r + 1)
                for kind, odd, power in ((0, 0, 1), (0, 1, 0), (1, 0, 0)):
                    for ri in range(2):
                        dst = near[:, kind, ri, :, :].rearrange("p a (m j c) -> p a m j c", j=2, c=SG)[:, :, :, odd, :]
                        src = Xp[:, ri, :, (7 - power) * SG:(8 - power) * SG].unsqueeze(2).to_broadcast([P, RP, 4, SG])
                        g.tensor_copy(dst, src).then_inc(s5_near, 1)
                gates_out(3 + 2 * r)
                gates_out(4 + 2 * r)

            def y_piece(pc):
                if pc >= 4:
                    pool.wait_ge(y_lo, pc - 3)
                b, half, k = pc // 8, pc % 8 // 4, pc % 4
                g.dma_start(yst[:, k, :], y_dram[b, k, :, half * 512:half * 512 + 512]).then_inc(y_loaded[k], 16)

            def gate_back(i):
                if i >= 4:
                    pool.wait_ge(merged, 2 * (i - 3))
                b = (0, 2, 1)[i // 8]
                g.dma_start(tok[:, (i % 4) * L:(i % 4 + 1) * L], g_dram[b, i % 8]).then_inc(gate_in[i % 4], 16)

            for s in range(2):
                pool.wait_ge(y_sent[s], 128)
            pool.wait_ge(s5_xs, 4)
            for pc in range(8):
                y_piece(pc)
            pool.wait_ge(gelu_done, 4)
            for s in range(2):
                pool.wait_ge(g_sent[s], 16 * 22)
            for i in range(4):
                gate_back(i)
            gates_out(11)
            for pc in range(8, 12):
                y_piece(pc)
            for i in range(4, 8):
                gate_back(i)
            y_piece(12)
            y_piece(13)
            for s in range(2):
                pool.wait_ge(g_sent[s], 16 * 24)
            gate_back(8)
            gate_back(9)
            y_piece(14)
            y_piece(15)
            for i in range(10, 24):
                gate_back(i)
            yx = yst[:, :, :].rearrange("p (s a) c -> p s (a c)", s=2)

            def x_load(t):
                g.dma_start(yx[:, t % 2, :], x[t * P:(t + 1) * P, :]).then_inc(x_back[t % 2], 16)

            pool.wait_ge(y_lo, 24)
            x_load(0)
            x_load(1)
            pool.wait_ge(merged, 42)
            g.dma_start(tok[:, 0:D], a["g_mix_post"][0].partition_broadcast(P)).then_inc(post_gains, 16)
            pool.wait_ge(merged, 44)
            g.dma_start(tok[:, D:2 * D], a["g_mlp_pre"][0].partition_broadcast(P)).then_inc(post_gains, 16)
            for t in range(NT):
                pool.wait_ge(x1_made, t + 1)
                g.dma_start(x1_dram[t * P:(t + 1) * P, :], yx[:, t % 2, :]).then_inc(x1_sent, 16)
                if t + 2 < NT:
                    pool.wait_ge(x1_sent, 16 * (t + 1))
                    pool.wait_ge(h2_made, t + 1)
                    x_load(t + 2)
            g.memset(acc[:, :, :], 0.0).then_inc(acc_zero, 1)
            g.dma_start(tok[:, 0:D], a["g_mlp_post"][0].partition_broadcast(P)).then_inc(last_gain, 16)
            pool.wait_ge(x1_sent, 16 * NT)
            pool.wait_ge(h2_made, NT)
            for e in range(2):
                wait_taken(pool, out_event("h", 7, e))

            def x1_load(t):
                g.dma_start(tok[:, (1 + t % 3) * D:(2 + t % 3) * D], x1_dram[t * P:(t + 1) * P, :]).then_inc(x1_back[t % 3], 16)

            for t in range(3):
                x1_load(t)
            for t in range(3, NT):
                pool.wait_ge(out_sent[t % 3], 16 * (t // 3))
                x1_load(t)

        @block.scalar
        def _(act):
            A = nc.scalar

            def copy_out(n, dst, src=None):
                wait_full(act, n)
                A.activation(dst, banks[n % 8][:, :] if src is None else src, ACT.Copy).then_inc(bank_free[n % 8], 1)

            def square(idx):
                if idx < 2:
                    act.wait_ge(mem_in[idx], 16)
                else:
                    act.wait_ge(tile_in[idx % 7], 32 if idx == 9 else 16)
                if idx:
                    act.wait_ge(square_sum, idx)
                A.activation(junk[:, :], xtile(idx), ACT.Square, accum_out=sumsq[:, idx:idx + 1]).then_inc(square_sum, 1)

            def norm_event(idx, e):
                return FIRST["front"] + (2 * idx + e if idx < 2 else 6 + 6 * ((idx - 2) // 2) + 2 * ((idx - 2) % 2) + e)

            def norm_hi(idx):
                for e in range(2):
                    n = norm_event(idx, e)
                    dst = (mThi[:, 4 * e:4 * e + 4, idx * P:(idx + 1) * P] if idx < 2
                           else hThi[:, 4 * e:4 * e + 4, (idx - 2) * P:(idx - 1) * P])
                    wait_full(act, n)
                    A.activation(dst, banks[n % 8][:, :].rearrange("p (k t) -> p k t", k=4), ACT.Copy).then_inc(split_hi, 1)

            square(0)
            square(1)
            prep_hi(act, 0, None)
            norm_hi(0)
            norm_hi(1)
            square(2)
            square(3)
            prep_hi(act, 1, None)
            square(4)
            square(5)
            for s in range(4):
                n0 = FIRST["front"] + 4 + 6 * s
                for i in range(2):
                    dst = kmT[:, 2 * s + i, :] if s < 2 else vm[:, i, (s - 2) * 256:(s - 1) * 256]
                    copy_out(n0 + i, dst, banks[(n0 + i) % 8][:, 0:256])
                prep_hi(act, s + 2, n0 + 1)
                norm_hi(2 + 2 * s)
                norm_hi(3 + 2 * s)
                if s < 2:
                    square(6 + 2 * s)
                    square(7 + 2 * s)
            tokq = tok[:, :].rearrange("p (i t) -> p i t", i=4)
            act.wait_ge(s5_small_in, 48)
            A.activation(sload[:, 2, :].rearrange("k (g p) -> k g p", g=2), ldt[:, :].unsqueeze(2).to_broadcast([NPAIR, 2, ST]),
                         ACT.Copy).then_inc(s5_dt, 1)
            n = FIRST["spar"]
            copy_out(n, spar[:, :, :].rearrange("p a b -> p (a b)"), banks[n % 8][:, 0:48])
            for s in range(2):
                n0 = FIRST["qx"] + 4 * s
                if s:
                    prep_hi(act, U_QX + s + 1, n0 - 1)
                for i in range(2):
                    for half in range(2):
                        copy_out(n0 + 2 * i + half, tokq[:, 2 * s + i, half * 512:half * 512 + 512])
                if s == 0:
                    act.wait_ge(trig_arg, 1)
                    act.wait_ge(consts, 6)
                    A.activation(cosT[:, :], cosT[:, :], ACT.Sin, scale=-1.0, bias=halfpi[:, 0:1]).then_inc(trig_done, 1)
                    A.activation(sinT[:, :], sinT[:, :], ACT.Sin).then_inc(trig_done, 1)
            act.wait_ge(s5_trig, 1)
            A.activation(small[:, 5, :], small[:, 5, :], ACT.Sin, scale=-1.0, bias=halfpi[:, 0:1]).then_inc(s5_trig_done, 1)
            A.activation(small[:, 4, :], small[:, 4, :], ACT.Sin).then_inc(s5_trig_done, 1)
            for e in range(16):
                wait_taken(act, FIRST["xsc"] + e)
                A.activation(prob[:, e, :], prob[:, e, :], ACT.Exp).then_inc(x_exp, 1)
            for s in range(2):
                n0 = FIRST["q"] + 4 * s
                prep_hi(act, U_Q + s + 1, n0 - 1)
                for i in range(2):
                    for half in range(2):
                        n = n0 + 2 * i + half
                        copy_out(n, qwin[:, s, i, 8 * half:8 * half + 8, :], banks[n % 8][:, :].rearrange("p (n c) -> p n c", c=CH))
            n0 = FIRST["kv"]
            prep_hi(act, U_KV + 1, n0 - 1)
            for i, dst in enumerate((kT, vT)):
                for half in range(2):
                    copy_out(n0 + 2 * i + half, dst[:, half * 512:half * 512 + 512])
            for q in range(8):
                for m in range(2):
                    copy_out(FIRST["xpv"] + pv_event(q, m), pT[:, q % 2, m, :])
            act.wait_ge(rope_done, 10)
            for e in range(4):
                copy_out(FIRST["vwin"] + e, vwin[:, 4 * e:4 * e + 4, :].rearrange("p n d -> p (n d)"))

            def gates(i, between=None):
                n0 = FIRST[f"g{i}"]
                prep_hi(act, U_GATE[i] + 1, n0 - 1)
                if between:
                    between()
                for gp in range(4 * i, 4 * i + 4):
                    n = n0 + gp % 4
                    if gp >= 2:
                        act.wait_ge(g_sent[gp % 2], 16 * (gp // 2))
                    wait_full(act, n)
                    A.activation(scr[:, gp % 2, :], banks[n % 8][:, :], ACT.Sigmoid).then_inc(bank_free[n % 8], 1)

            gates(0)
            for e in range(16):
                act.wait_ge(sink_arg, e + 1)
                pe4 = prob[:, e, :].rearrange("p (s k) -> p s k", s=4)
                if e < 2:
                    A.activation(pe4[:, 0:2, 0:64], pe4[:, 0:2, 0:64], ACT.Exp)
                    A.activation(pe4[:, 2:4, :], pe4[:, 2:4, :], ACT.Exp).then_inc(s_exp, 1)
                else:
                    A.activation(prob[:, e, :], prob[:, e, :], ACT.Exp).then_inc(s_exp, 1)
            A.activation(sinkx[:, :, :], sinkx[:, :, :], ACT.Exp).then_inc(sink_exp, 1)
            for s in range(2):
                n0 = FIRST["u"] + 4 * s
                prep_hi(act, U_U + s + 1, n0 - 1)
                for jj in range(4):
                    n = n0 + jj
                    src = banks[n % 8][:, :].rearrange("p (j g c) -> p j g c", j=2, c=SG)
                    copy_out(n, uc[:, 16 * s:16 * s + 16, 2 * jj:2 * jj + 2, :].rearrange("p g j c -> p j g c"), src)
            gates(1)
            for q in range(8):
                for nn in range(2):
                    n = FIRST["spv"] + pv_event(q, nn)
                    nk = 64 if q == 0 and nn == 0 else P
                    copy_out(n, pT[0:nk, q % 2, nn, :], banks[n % 8][0:nk, :])
            gates(2)
            for ri in range(2):
                n = FIRST["spc"] + ri
                wait_full(act, n)
                src = banks[n % 8][:, :].rearrange("p (k g o) -> p g k o", g=2, o=SG)
                A.activation(cpk[0:64, ri, :, :], src[0:64, 0, :, :], ACT.Copy)
                A.activation(cpk[64:P, ri, :, :], src[64:P, 1, :, :], ACT.Copy).then_inc(bank_free[n % 8], 1)
            for r in range(4):
                n0 = FIRST[f"s5a{r}"]
                for e in range(2):
                    copy_out(n0 + e, uT[:, 4 * e:4 * e + 4, :].rearrange("p g c -> p (g c)"))
                for ri in range(2):
                    copy_out(n0 + 2 + ri, wT[:, ri, :, :].rearrange("p g c -> p (g c)"))
                gates(3 + 2 * r)
                for e in range(2):
                    n = FIRST[f"s5m{r}"] + e
                    wait_full(act, n)
                    for m in range(4):
                        rows = slice(32 * m, 32 * m + 32)
                        src = banks[n % 8][rows, :].rearrange("p (b x) -> p b x", b=4)[:, :, 0:P - 32 * m]
                        ins = A.activation(Mt[rows, 4 * e:4 * e + 4, 32 * m:P], src, ACT.Copy)
                    ins.then_inc(bank_free[n % 8], 1)
                gates(4 + 2 * r)

            def y_piece(pc, hi):
                half, k = pc % 8 // 4, pc % 4
                act.wait_ge(y_loaded[k], 16 * (pc // 4 + 1))
                A.activation(hi[:, k, half * 512:half * 512 + 512], yst[:, k, :], ACT.Copy).then_inc(y_hi, 1)

            def gelu():
                for e in range(2):
                    wait_taken(act, FIRST["s5y3"] + e)
                for r in range(4):
                    A.activation(gl[r].rearrange("p i (g c) -> p g i c", c=SG), uc[:, 8 * r:8 * r + 8, :, :],
                                 ACT.Gelu_apprx_tanh).then_inc(gelu_done, 1)
                for pc in range(8):
                    y_piece(pc, yhi)

            gates(11, gelu)
            for e in range(8):
                n = FIRST["yg"] + e
                dst = hThi[:, e // 2, :].rearrange("p (c i) -> p i c", i=STEP)[:, 4 * (e % 2):4 * (e % 2) + 4, :]
                wait_full(act, n)
                A.activation(dst, banks[n % 8][:, :].rearrange("p (i c) -> p i c", i=4), ACT.Copy).then_inc(split_hi, 1)
            for s in range(2):
                prep_hi(act, U_MERGE_A + s + 1, FIRST["mergeA"] - 9 if s == 0 else FIRST["mergeA"] + 7)
                for pc in range(8 + 4 * s, 12 + 4 * s):
                    y_piece(pc, hThi[:, 4:8, :])
            for s in range(2):
                act.wait_ge(g_sent[s], 16 * 24)
            for s in range(2):
                n0 = FIRST["glu"] + 8 * s
                prep_hi(act, U_GLU + s + 1, n0 - 1)
                for j in range(4):
                    n = n0 + 2 * j + 1
                    wait_full(act, n)
                    A.activation(scr[:, j % 2, :], banks[n % 8][:, :], ACT.Sigmoid).then_inc(bank_free[n % 8], 1)
                    wait_taken(act, n - 1)
                    A.activation(yhi[:, 2 * s + j // 2, (j % 2) * 512:(j % 2) * 512 + 512], yst[:, j, :], ACT.Copy).then_inc(y_hi, 1)
            for s in range(2):
                prep_hi(act, U_MERGE_M + s + 1, FIRST["mergeM"] + 8 * s - 1)
            for s in range(2):
                prep_hi(act, U_MERGE_S + s + 1, FIRST["mergeS"] + 8 * s - 1)
                for k in range(4 * s, 4 * s + 4):
                    act.wait_ge(merged, 32 + 2 * k + 2)
                    A.activation(hThi[:, k, :], acc[:, k, :], ACT.Copy).then_inc(m_hi, 1)
            for s in range(1, 4):
                prep_hi(act, U_OUT + s, FIRST["out"] - 1)
            yx = yst[:, :, :].rearrange("p (s a) c -> p s (a c)", s=2)
            flat = scr[:, :, :].rearrange("p a c -> p (a c)")

            squares = {"o": 0, "x": 0}

            def square2(kind, src, column):
                if squares["o"]:
                    act.wait_ge(sq_o, squares["o"])
                if squares["x"]:
                    act.wait_ge(sq_x, squares["x"])
                squares[kind] += 1
                A.activation(flat, src, ACT.Square, accum_out=sumsq[:, column:column + 1]).then_inc(sq_o if kind == "o" else sq_x, 1)

            def square_o(t):
                square2("o", acc[:, t, :], 10 + t)

            def h2_hi(t):
                for e in range(2):
                    n = out_event("h", t, e)
                    wait_full(act, n)
                    A.activation(hThi[:, 4 * e:4 * e + 4, t * P:(t + 1) * P],
                                 banks[n % 8][:, :].rearrange("p (k t) -> p k t", k=4), ACT.Copy).then_inc(split_hi, 1)

            def square_x(t):
                act.wait_ge(x1_made, t + 1)
                square2("x", yx[:, t % 2, :], 18 + t)

            for step in OUT_ORDER:
                t = int(step[1])
                if step[0] == "w":
                    for e in range(2):
                        copy_out(out_event("w", t, e), acc[:, t, e * 512:e * 512 + 512])
                        if t == 7 and e == 0:
                            prep_hi(act, U_MLP, out_event("w", 7, 0))
                    for e in range(2):
                        wait_taken(act, out_event("w", t, e))
                    square_o(t)
                    if t:
                        square_x(t - 1)
                else:
                    h2_hi(t)
                    if t == 5:
                        square_x(NT - 1)

            def mlp(it, first, last):
                for s in range(2):
                    n0 = FIRST["mlp"] + 4 * s
                    prep_hi(act, U_MLP + s + 1, out_event("w", 7, 0) if first and s == 0 else n0 - 1, it, 4, 24)
                    for j in range(4):
                        n, pc = n0 + j, 4 * s + j
                        wait_full(act, n, it, 24)
                        A.activation(scr[:, pc % 2, :], banks[n % 8][:, :], ACT.Relu).then_inc(bank_free[n % 8], 1)
                        act.wait_ge(f_sq, it * 8 + pc + 1)
                        A.activation(yhi[:, 2 * s + j % 2, (j // 2) * 512:(j // 2) * 512 + 512], yst[:, pc % 4, :],
                                     ACT.Copy).then_inc(f_hi, 1)
                prep_hi(act, U_MLP + 3, FIRST["mlp"] + 7, it, 4, 24)
                if not last:
                    prep_hi(act, U_MLP + 4, FIRST["mlp"] + 15, it, 4, 24)

            mlp(0, True, False)
            with act.Fori(1, 7) as it:
                mlp(it, False, False)
            mlp(7, False, True)
            for t in range(NT):
                act.wait_ge(acc_done, t + 1)
                square2("o", acc[:, t, :], 26 + t)

        @block.vector
        def _(dve):
            V = nc.vector
            issued = [0]

            def mark(ins):
                issued[0] += 1
                ins.then_inc(chain, 1)

            def settle():
                dve.wait_ge(chain, issued[0])

            def do(ins):
                mark(ins)
                settle()

            def rstd(src):
                mark(V.tensor_scalar(stat[:, 0:1], src, 1.0 / D, EPS, mul, add))
                mark(V.tensor_scalar(stat[:, 3:4], src, -0.5 / D, -0.5 * EPS, mul, add))
                settle()
                do(V.tensor_scalar(stat[:, 1:2].bitcast(i32), stat[:, 0:1].bitcast(i32), -0.5, RSQRT_SEED, mul, add))
                for _ in range(3):
                    do(V.scalar_tensor_tensor(out=stat[:, 2:3], in0=stat[:, 1:2], scalar=stat[:, 3:4], in1=stat[:, 1:2], op0=mul, op1=mul))
                    do(V.scalar_tensor_tensor(out=stat[:, 1:2], in0=stat[:, 2:3], scalar=1.5, in1=stat[:, 1:2], op0=add, op1=mul))

            def reduce_angle(x, k):
                do(V.tensor_scalar(k, x, float(np.float32(1 / (2 * np.pi))), MAGIC, mul, add))
                do(V.tensor_scalar(k, k, MAGIC, None, sub))
                for c in TWO_PI:
                    do(V.scalar_tensor_tensor(out=x, in0=k, scalar=-c, in1=x, op0=mul, op1=add))
                do(V.tensor_scalar(x, x, PI_DOWN, -PI_DOWN, ALU.min, ALU.max))
                do(V.scalar_tensor_tensor(out=k, in0=x, scalar=-1.0, in1=x, op0=mul, op1=ALU.max))

            def cmul(o, x, y, t):
                mark(V.tensor_tensor(t[0], x[0], y[0], mul))
                mark(V.tensor_tensor(t[1], x[1], y[1], mul))
                mark(V.tensor_tensor(t[2], x[0], y[1], mul))
                mark(V.tensor_tensor(t[3], x[1], y[0], mul))
                settle()
                mark(V.tensor_tensor(o[0], t[0], t[1], sub))
                mark(V.tensor_tensor(o[1], t[2], t[3], add))
                settle()

            def norm_event(idx, e):
                return FIRST["front"] + (2 * idx + e if idx < 2 else 6 + 6 * ((idx - 2) // 2) + 2 * ((idx - 2) % 2) + e)

            def rstd2(pair):
                c = slice(2 * pair, 2 * pair + 2)
                y, v, nv, t = rs[:, c], stat[:, 0:2], stat[:, 2:4], stat[:, 4:6]
                dve.wait_ge(square_sum, 2 * pair + 2)
                mark(V.tensor_scalar(v, sumsq[:, c], 1.0 / D, EPS, mul, add))
                mark(V.tensor_scalar(nv, sumsq[:, c], -0.5 / D, -0.5 * EPS, mul, add))
                settle()
                do(V.tensor_scalar(y.bitcast(i32), v.bitcast(i32), -0.5, RSQRT_SEED, mul, add))
                for _ in range(3):
                    do(V.tensor_tensor(t, y, y, mul))
                    do(V.tensor_tensor(t, t, nv, mul))
                    do(V.scalar_tensor_tensor(out=y, in0=t, scalar=1.5, in1=y, op0=add, op1=mul))

            def norm_h(idx):
                if idx >= 2:
                    for e in range(2):
                        wait_full(dve, norm_event(idx - 2, e))
                if idx in (0, 2):
                    dve.wait_ge(gain2_in if idx else gains_in, 16)
                V.scalar_tensor_tensor(out=hst[:, idx % 2, :], in0=xtile(idx), scalar=rs[:, idx:idx + 1],
                                       in1=(gmem if idx < 2 else gpre)[:, :], op0=mul, op1=mul).then_inc(h_made, 1)

            def norm_lo(idx):
                for e in range(2):
                    n = norm_event(idx, e)
                    sl = (slice(None), slice(4 * e, 4 * e + 4), slice((idx % 2) * P, (idx % 2) * P + P) if idx < 2
                          else slice((idx - 2) * P, (idx - 1) * P))
                    hi, lo = (mThi, mTlo) if idx < 2 else (hThi, hTlo)
                    dve.wait_ge(split_hi, 2 * idx + e + 1)
                    V.tensor_tensor(lo[sl], banks[n % 8][:, :].rearrange("p (k t) -> p k t", k=4), hi[sl].bitcast(f32), sub)\
                        .then_inc(bank_free[n % 8], 1)

            rstd2(0)
            norm_h(0)
            norm_h(1)
            prep_lo(dve, 0)
            norm_lo(0)
            norm_lo(1)
            rstd2(1)
            norm_h(2)
            norm_h(3)
            prep_lo(dve, 1)
            for s in range(4):
                if s < 3:
                    rstd2(s + 2)
                    norm_h(4 + 2 * s)
                norm_lo(2 + 2 * s)
                if s < 3:
                    norm_h(5 + 2 * s)
                norm_lo(3 + 2 * s)
                prep_lo(dve, s + 2)
            dve.wait_ge(pos_in, 32)
            dve.wait_ge(h_made, 10)
            do(V.tensor_scalar(sinT[:, :], yst2[:, :, :].rearrange("p a b -> p (a b)").bitcast(i32), stat[:, 7:8], None, mul))
            reduce_angle(sinT[:, :], cosT[:, :])
            dve.sem_inc(trig_arg, 1)
            sm = [small[:, k, :] for k in range(12)]

            def exp_exact(o, x, t):
                k, r, pw = t
                do(V.tensor_scalar(r, x, 200.0, -200.0, ALU.min, ALU.max))
                do(V.tensor_scalar(k, r, float(np.float32(1 / np.log(2.0))), MAGIC, mul, add))
                do(V.tensor_scalar(k, k, MAGIC, None, sub))
                do(V.tensor_scalar(k, k, 128.0, -127.0, ALU.min, ALU.max))
                for c in LN2:
                    do(V.scalar_tensor_tensor(out=r, in0=k, scalar=-c, in1=r, op0=mul, op1=add))
                do(V.tensor_scalar(smalli[:, :], k, 127.0, 8388608.0, add, mul))
                fact = [1.0]
                for q in range(1, 8):
                    fact.append(fact[-1] * q)
                do(V.tensor_scalar(pw, r, 1.0 / fact[7], None, mul))
                for q in range(6, 0, -1):
                    do(V.scalar_tensor_tensor(out=pw, in0=pw, scalar=1.0 / fact[q], in1=r, op0=add, op1=mul))
                do(V.scalar_tensor_tensor(out=o, in0=pw, scalar=1.0, in1=smalli[:, :].bitcast(f32), op0=add, op1=mul))

            wait_taken(dve, FIRST["spar"])
            a_re, a_im, log_dt = spar[:, 0, :], spar[:, 1, :], spar[:, 2, :]
            exp_exact(sm[0], log_dt, sm[1:4])
            do(V.tensor_tensor(sm[4], a_im, sm[0], mul))
            do(V.tensor_tensor(sm[6], a_re, sm[0], mul))
            reduce_angle(sm[4], sm[5])
            dve.sem_inc(s5_trig, 1)
            exp_exact(sm[6], sm[6], sm[1:4])
            prep_lo(dve, U_QX + 2)
            XS = float(P) ** -0.5
            for e in range(16):
                n = FIRST["xsc"] + e
                ps = banks[n % 8][:, :].rearrange("p (h m) -> p h m", h=2)
                wait_full(dve, n)
                m2 = mx[:, 2 * e:2 * e + 2]
                do(V.reduce_max(m2, ps, AX.X))
                do(V.tensor_scalar(m2, m2, XS, None, mul))
                V.scalar_tensor_tensor(out=prob[:, e, :].rearrange("p (h m) -> p h m", h=2), in0=ps, scalar=XS,
                                       in1=m2.unsqueeze(2).to_broadcast([P, 2, MEM]), op0=mul, op1=sub).then_inc(bank_free[n % 8], 1)

            def x_normalise(e):
                pe2 = prob[:, e, :].rearrange("p (h m) -> p h m", h=2)
                d2 = den[:, 2 * e:2 * e + 2]
                dve.wait_ge(x_exp, e + 1)
                do(V.reduce_sum(d2, pe2, AX.X))
                do(V.reciprocal(d2, d2))
                V.tensor_tensor(pe2, pe2, d2.unsqueeze(2).to_broadcast([P, 2, MEM]), mul).then_inc(x_prob, 1)

            prep_lo(dve, U_Q + 1)
            for e in range(8):
                x_normalise(e)
            prep_lo(dve, U_Q + 2)
            for e in range(8, 16):
                x_normalise(e)
            prep_lo(dve, U_KV + 1)
            temps = (mx, den, sinkx[:, :, :].rearrange("p a b -> p (a b)"), small[:, 8:12, :].rearrange("p a b -> p (a b)"))
            dve.wait_ge(s5_trig_done, 2)
            sin, cos, mag = sm[4], sm[5], sm[6]
            do(V.memset(pwF[:, 0, :, 0:1], 1.0))
            do(V.memset(pwF[:, 1, :, 0:1], 0.0))
            do(V.tensor_tensor(pwF[:, 0, :, 1], mag, cos, mul))
            do(V.tensor_tensor(pwF[:, 1, :, 1], mag, sin, mul))
            for k in (1, 2, 4):
                o = [pwF[:, ri, :, k + 1:2 * k + 1] for ri in range(2)]
                x = [pwF[:, ri, :, 1:k + 1] for ri in range(2)]
                y = [pwF[:, ri, :, k].unsqueeze(2).to_broadcast([P, NPAIR, k]) for ri in range(2)]
                t = [tt[:, 0:NPAIR * k].rearrange("p (a b) -> p a b", b=k) for tt in temps]
                cmul(o, x, y, t)
            for j in range(8):
                mark(V.tensor_copy(pwR[:, :, :, j], pwF[:, :, :, 7 - j]))
            settle()
            do(V.tensor_tensor(sm[1], a_re, a_re, mul))
            do(V.tensor_tensor(sm[2], a_im, a_im, mul))
            do(V.tensor_tensor(sm[1], sm[1], sm[2], add))
            do(V.reciprocal(sm[1], sm[1]))
            do(V.tensor_scalar(sm[2], pwF[:, 0, :, 1], 1.0, None, sub))
            n_im = pwF[:, 1, :, 1]
            do(V.tensor_tensor(sm[7], sm[2], a_re, mul))
            do(V.tensor_tensor(sm[8], n_im, a_im, mul))
            do(V.tensor_tensor(sm[7], sm[7], sm[8], add))
            do(V.tensor_tensor(sm[7], sm[7], sm[1], mul))
            do(V.tensor_tensor(sm[8], n_im, a_re, mul))
            do(V.tensor_tensor(sm[9], sm[2], a_im, mul))
            do(V.tensor_tensor(sm[8], sm[8], sm[9], sub))
            do(V.tensor_tensor(sm[8], sm[8], sm[1], mul))
            do(V.tensor_tensor(rho[:, :], mag, mag, mul))
            do(V.tensor_tensor(rho[:, :], rho[:, :], rho[:, :], mul))
            do(V.tensor_tensor(rho[:, :], rho[:, :], rho[:, :], mul))
            t16 = [mx[:, 0:16], mx[:, 16:32], den[:, 0:16], den[:, 16:32]]
            cur = [cos, sin]
            for k in range(3 + 6):
                nxt = ([sm[9], sm[10]] if k % 2 == 0 else [sm[1], sm[2]]) if k < 2 else [rotF[:, ri, k - 2, :] for ri in range(2)]
                cmul(nxt, cur, cur, t16)
                cur = nxt
            for q in range(8):
                n = FIRST["xpv"] + pv_event(q, 2)
                wait_full(dve, n)
                if q >= 2:
                    dve.wait_ge(y_sent[q % 2], 16 * (q // 2))
                V.tensor_copy(yst2[:, q % 2, :], banks[n % 8][:, :]).then_inc(bank_free[n % 8], 1)
            dve.wait_ge(trig_done, 2)
            for e in range(10):
                n = FIRST["rope"] + e
                half = slice((e % 2) * 512, (e % 2) * 512 + 512)
                by_chunk = lambda v: v.rearrange("p (n c) -> p n c", c=CH)
                qk = qwin[:, e // 4, (e // 2) % 2, 8 * (e % 2):8 * (e % 2) + 8, :] if e < 8 else by_chunk(kT[:, half])
                wait_full(dve, n)
                mark(V.tensor_tensor(scr[:, e % 2, :], banks[n % 8][:, :], sinT[:, half], mul))
                mark(V.tensor_tensor(qk, qk, by_chunk(cosT[:, half]), mul))
                settle()
                V.tensor_tensor(qk, qk, by_chunk(scr[:, e % 2, :]), add).then_inc(rope_done, 1)
                dve.sem_inc(bank_free[n % 8], 1)
            prep_lo(dve, U_GATE[0] + 1)
            SS = float(HD) ** -0.5
            dve.wait_ge(sinks_in, 32)
            for e in range(16):
                n = FIRST["ssc"] + e
                j = e % 2
                ps = banks[n % 8][:, :].rearrange("p (s k) -> p s k", s=4)
                pe4 = prob[:, e, :].rearrange("p (s k) -> p s k", s=4)
                parts = [(0, 2, 64), (2, 4, P)] if e < 2 else [(0, 4, P)]
                m4 = mx[:, 4 * e:4 * e + 4]
                wait_full(dve, n)
                for lo, hi, nk in parts:
                    mark(V.reduce_max(m4[:, lo:hi], ps[:, lo:hi, 0:nk], AX.X))
                settle()
                sk = sinkb[:, 2 * j:2 * j + 2].unsqueeze(1).to_broadcast([P, 2, 2])
                do(V.scalar_tensor_tensor(out=m4.rearrange("p (s a) -> p s a", s=2), in0=m4.rearrange("p (s a) -> p s a", s=2),
                                          scalar=SS, in1=sk, op0=mul, op1=ALU.max))
                for lo, hi, nk in parts:
                    ins = V.scalar_tensor_tensor(out=pe4[:, lo:hi, 0:nk], in0=ps[:, lo:hi, 0:nk], scalar=SS,
                                                 in1=m4[:, lo:hi].unsqueeze(2).to_broadcast([P, hi - lo, nk]), op0=mul, op1=sub)
                ins.then_inc(bank_free[n % 8], 1)
                V.tensor_tensor(sinkx[:, e, :].rearrange("p (s a) -> p s a", s=2), sk,
                                m4.rearrange("p (s a) -> p s a", s=2), sub).then_inc(sink_arg, 1)

            def s_normalise(e):
                pe4 = prob[:, e, :].rearrange("p (s k) -> p s k", s=4)
                parts = [(0, 2, 64), (2, 4, P)] if e < 2 else [(0, 4, P)]
                d4 = den[:, 4 * e:4 * e + 4]
                for lo, hi, nk in parts:
                    mark(V.reduce_sum(d4[:, lo:hi], pe4[:, lo:hi, 0:nk], AX.X))
                settle()
                do(V.tensor_tensor(d4, d4, sinkx[:, e, :], add))
                do(V.reciprocal(d4, d4))
                for lo, hi, nk in parts:
                    ins = V.tensor_tensor(pe4[:, lo:hi, 0:nk], pe4[:, lo:hi, 0:nk],
                                          d4[:, lo:hi].unsqueeze(2).to_broadcast([P, hi - lo, nk]), mul)
                ins.then_inc(s_prob, 1)

            dve.wait_ge(sink_exp, 1)
            prep_lo(dve, U_U + 1)
            for e in range(16):
                s_normalise(e)
            prep_lo(dve, U_U + 2)
            prep_lo(dve, U_GATE[1] + 1)
            for q in range(8):
                n = FIRST["spv"] + pv_event(q, 2)
                wait_full(dve, n)
                dve.wait_ge(y_sent[q % 2], 16 * (q // 2 + 4))
                V.tensor_copy(yst2[:, q % 2, :].rearrange("p (i s t) -> p s i t", i=4, s=2),
                              banks[n % 8][:, :].rearrange("p (s i t) -> p s i t", s=2, i=4)).then_inc(bank_free[n % 8], 1)
            do(V.memset(near[:, 1, :, :, :], 0.0))
            do(V.memset(Mt[:, :, :], 0.0))
            do(V.memset(ca[:, :, :, :], 0.0))
            do(V.memset(xs[:, :, :, 0:1], 0.0))
            prep_lo(dve, U_GATE[2] + 1)
            dve.wait_ge(s5_in, 112)
            temps = (t1, t2, t3, t4)
            cmul([Bb[:, ri, :, :] for ri in range(2)], [sm[7 + ri].unsqueeze(2).to_broadcast([P, NPAIR, SG]) for ri in range(2)],
                 [sB[:, ri, :, :] for ri in range(2)], [tt[:, 0:256].rearrange("p (a b) -> p a b", b=SG) for tt in temps])
            t512 = [tt[:, :].rearrange("p (a b c) -> p a b c", a=RP, b=8) for tt in temps]

            def make_x(r):
                pr = slice(RP * r, RP * r + RP)
                if r:
                    dve.wait_ge(s5_near, 6 * r)
                cmul([Xp[:, ri, :, 0:P].rearrange("p a (b c) -> p a b c", b=8) for ri in range(2)],
                     [pwR[:, ri, pr, :].unsqueeze(3).to_broadcast([P, RP, 8, SG]) for ri in range(2)],
                     [Bb[:, ri, pr, :].unsqueeze(2).to_broadcast([P, RP, 8, SG]) for ri in range(2)], t512)
                dve.sem_inc(s5_x, 1)

            make_x(0)
            for ri in range(2):
                wait_taken(dve, FIRST["spc"] + ri)
            for r in range(4):
                pr = slice(RP * r, RP * r + RP)
                ap = [pwF[:, ri, pr, 1:9].unsqueeze(3).to_broadcast([P, RP, 8, SG]) for ri in range(2)]
                cc = [cpk[:, ri, pr, :].unsqueeze(2).to_broadcast([P, RP, 8, SG]) for ri in range(2)]
                cav = [ca[:, ri, :, :].rearrange("p a (g b c) -> p a g b c", g=2, b=9) for ri in range(2)]
                for k, (x, y) in enumerate(((0, 0), (1, 1), (0, 1), (1, 0))):
                    mark(V.tensor_tensor(t512[k], ap[x], cc[y], mul))
                settle()
                for gg in range(2):
                    s = slice(64 * gg, 64 * gg + 64)
                    mark(V.tensor_copy(cav[0][s, :, gg, 0, :], cpk[s, 0, pr, :]))
                    mark(V.tensor_scalar(cav[1][s, :, gg, 0, :], cpk[s, 1, pr, :], -1.0, None, mul))
                    mark(V.tensor_tensor(cav[0][s, :, gg, 1:9, :], t512[0][s], t512[1][s], sub))
                    mark(V.scalar_tensor_tensor(out=cav[1][s, :, gg, 1:9, :], in0=t512[2][s], scalar=-1.0, in1=t512[3][s], op0=mul, op1=sub))
                settle()
                dve.sem_inc(s5_ca, 1)
                mark(V.memset(E[:, 0, :, 0:1], 1.0))
                mark(V.memset(E[:, 1, :, 0:1], 0.0))
                mark(V.tensor_copy(E[:, :, :, 1], rotF[:, :, 0, pr]))
                settle()
                for k in range(1, 7):
                    w = 1 << k
                    cmul([E[:, ri, :, w:2 * w] for ri in range(2)], [E[:, ri, :, 0:w] for ri in range(2)],
                         [rotF[:, ri, k, pr].unsqueeze(2).to_broadcast([P, RP, w]) for ri in range(2)],
                         [tt[:, 0:RP * w].rearrange("p (a b) -> p a b", a=RP) for tt in temps])
                prep_lo(dve, U_GATE[3 + 2 * r] + 1)
                for e in range(2):
                    n = FIRST[f"s5a{r}"] + 4 + e
                    wait_full(dve, n)
                    q = slice(2 * e, 2 * e + 2)
                    w = [banks[n % 8][:, :].rearrange("p (a ri c) -> p ri a c", a=2, ri=2)[:, ri] for ri in range(2)]
                    t = [tt[:, 256 * e:256 * e + 256].rearrange("p (a b) -> p a b", a=2) for tt in temps]
                    for k, (x, y) in enumerate(((0, 0), (1, 1), (1, 0), (0, 1))):
                        mark(V.tensor_tensor(t[k], w[x], E[:, y, q, :], mul))
                    settle()
                    mark(V.tensor_tensor(v5[:, 0, q, :], t[0], t[1], add))
                    mark(V.tensor_tensor(v5[:, 1, q, :], t[2], t[3], sub))
                    dve.sem_inc(bank_free[n % 8], 1)
                settle()
                for ri in range(2):
                    for q in range(RP):
                        mark(V.tensor_tensor_scan(z5[:, ri, q, :], rho[:, RP * r + q:RP * r + q + 1].to_broadcast([P, NC8]),
                                                  v5[:, ri, q, :], 0.0, mul, add))
                settle()
                c127 = NC8 - 1
                cmul([xs[:, ri, :, 1:NC8] for ri in range(2)], [E[:, ri, :, 0:c127] for ri in range(2)],
                     [z5[:, ri, :, 0:c127] for ri in range(2)],
                     [tt[:, 0:RP * c127].rearrange("p (a b) -> p a b", a=RP) for tt in temps])
                dve.sem_inc(s5_xs, 1)
                if r < 3:
                    make_x(r + 1)
                prep_lo(dve, U_GATE[4 + 2 * r] + 1)
                dve.wait_ge(s5_du, r + 1)
                for e in range(2):
                    n = FIRST[f"s5y{r}"] + e
                    dst = uc[:, 8 * r + 4 * e:8 * r + 4 * e + 4, :, :].rearrange("p g i o -> p (g i o)")
                    wait_full(dve, n)
                    V.tensor_tensor(dst, banks[n % 8][:, :], dst, add).then_inc(bank_free[n % 8], 1)
            prep_lo(dve, U_GATE[11] + 1)

            def y_piece(pc, hi, lo):
                half, k = pc % 8 // 4, pc % 4
                h = slice(half * 512, half * 512 + 512)
                dve.wait_ge(y_hi, pc + 1)
                V.tensor_tensor(lo[:, k, h], yst[:, k, :], hi[:, k, h].bitcast(f32), sub).then_inc(y_lo, 1)

            for pc in range(8):
                y_piece(pc, yhi, ylo)
            for e in range(8):
                n = FIRST["yg"] + e
                sl = [y[:, e // 2, :].rearrange("p (c i) -> p i c", i=STEP)[:, 4 * (e % 2):4 * (e % 2) + 4, :] for y in (hThi, hTlo)]
                dve.wait_ge(split_hi, 20 + e + 1)
                V.tensor_tensor(sl[1], banks[n % 8][:, :].rearrange("p (i c) -> p i c", i=4), sl[0].bitcast(f32), sub).then_inc(bank_free[n % 8], 1)
            for s in range(2):
                prep_lo(dve, U_MERGE_A + s + 1)
                for j in range(8):
                    n, d, h = FIRST["mergeA"] + 8 * s + j, 4 * s + j // 2, slice((j % 2) * 512, (j % 2) * 512 + 512)
                    if j % 2 == 0:
                        dve.wait_ge(gate_in[d % 4], 16 * (s + 1))
                    wait_full(dve, n)
                    V.tensor_tensor(acc[:, d, h], banks[n % 8][:, :], tok[:, (d % 4) * L + h.start:(d % 4) * L + h.stop], mul)\
                        .then_inc(merged, 1)
                    dve.wait_ge(merged, 8 * s + j + 1)
                    dve.sem_inc(bank_free[n % 8], 1)
                    if s:
                        y_piece(8 + j, hThi[:, 4:8, :], hTlo[:, 4:8, :])
            for s in range(2):
                prep_lo(dve, U_GLU + s + 1)
                for j in range(4):
                    n = FIRST["glu"] + 8 * s + 2 * j
                    h = slice((j % 2) * 512, (j % 2) * 512 + 512)
                    wait_full(dve, n)
                    wait_taken(dve, n + 1)
                    V.tensor_tensor(yst[:, j, :], banks[n % 8][:, :], scr[:, j % 2, :], mul).then_inc(bank_free[n % 8], 1)
                    dve.wait_ge(y_hi, 16 + 4 * s + j + 1)
                    V.tensor_tensor(ylo[:, 2 * s + j // 2, h], yst[:, j, :], yhi[:, 2 * s + j // 2, h].bitcast(f32), sub).then_inc(y_lo, 1)

            def m_lo_part(k):
                dve.wait_ge(m_hi, k + 1)
                V.tensor_tensor(hTlo[:, k, :], acc[:, k, :], hThi[:, k, :].bitcast(f32), sub).then_inc(m_lo, 1)

            for b, (stage, u) in enumerate((("mergeM", U_MERGE_M), ("mergeS", U_MERGE_S))):
                dve.wait_ge(merged, 16 * (b + 1))
                for s in range(2):
                    prep_lo(dve, u + s + 1)
                    for j in range(8):
                        n, d, h = FIRST[stage] + 8 * s + j, 4 * s + j // 2, slice((j % 2) * 512, (j % 2) * 512 + 512)
                        if j % 2 == 0:
                            dve.wait_ge(gate_in[d % 4], 16 * (3 + 2 * b + s))
                        wait_full(dve, n)
                        V.tensor_tensor(scr[:, j % 2, :], banks[n % 8][:, :], tok[:, (d % 4) * L + h.start:(d % 4) * L + h.stop], mul)\
                            .then_inc(bank_free[n % 8], 1)
                        wait_taken(dve, n)
                        V.tensor_tensor(acc[:, d, h], acc[:, d, h], scr[:, j % 2, :], add).then_inc(merged, 1)
                        if b and j % 2 and d:
                            m_lo_part(d - 1)
            m_lo_part(KT - 1)
            for s in range(1, 4):
                prep_lo(dve, U_OUT + s)
            yx = yst[:, :, :].rearrange("p (s a) c -> p s (a c)", s=2)

            def residual(t):
                for e in range(2):
                    wait_taken(dve, out_event("w", t, e))
                scaled = acc[:, (t + 4) % NT, :]
                mark(V.tensor_tensor(scaled, acc[:, t, :], tok[:, 0:D], mul))
                dve.wait_ge(sq_o, t + 1)
                rstd(sumsq[:, 10 + t:11 + t])
                dve.wait_ge(x_back[t % 2], 16 * (t // 2 + 1))
                V.scalar_tensor_tensor(out=yx[:, t % 2, :], in0=scaled, scalar=stat[:, 1:2], in1=yx[:, t % 2, :], op0=mul, op1=add)\
                    .then_inc(x1_made, 1)

            def h2(t):
                dve.wait_ge(sq_x, t + 1)
                if t >= 2:
                    wait_full(dve, out_event("h", t - 2, 0))
                    wait_full(dve, out_event("h", t - 2, 1))
                rstd(sumsq[:, 18 + t:19 + t])
                V.scalar_tensor_tensor(out=tok[:, (2 + t % 2) * D:(3 + t % 2) * D], in0=yx[:, t % 2, :], scalar=stat[:, 1:2],
                                       in1=tok[:, D:2 * D], op0=mul, op1=mul).then_inc(h2_made, 1)

            def h2_lo(t):
                for e in range(2):
                    n = out_event("h", t, e)
                    sl = (slice(None), slice(4 * e, 4 * e + 4), slice(t * P, (t + 1) * P))
                    dve.wait_ge(split_hi, 28 + 2 * t + e + 1)
                    V.tensor_tensor(hTlo[sl], banks[n % 8][:, :].rearrange("p (k t) -> p k t", k=4), hThi[sl].bitcast(f32), sub)\
                        .then_inc(bank_free[n % 8], 1)

            dve.wait_ge(post_gains, 32)
            for step in OUT_ORDER:
                t = int(step[1])
                if step[0] == "w":
                    if t == 7:
                        prep_lo(dve, U_MLP)
                    residual(t)
                    if t:
                        h2(t - 1)
                else:
                    h2_lo(t)
                    if t == 5:
                        h2(NT - 1)
            dve.wait_ge(x1_sent, 16 * NT)

            def mlp(it, first, last):
                for s in range(2):
                    prep_lo(dve, U_MLP + s + 1, it, 4)
                    for j in range(4):
                        n, pc = FIRST["mlp"] + 4 * s + j, 4 * s + j
                        ct, h = 2 * s + j % 2, slice((j // 2) * 512, (j // 2) * 512 + 512)
                        wait_taken(dve, n, it, 24)
                        V.tensor_tensor(yst[:, pc % 4, :], scr[:, pc % 2, :], scr[:, pc % 2, :], mul).then_inc(f_sq, 1)
                        dve.wait_ge(f_hi, it * 8 + pc + 1)
                        V.tensor_tensor(ylo[:, ct, h], yst[:, pc % 4, :], yhi[:, ct, h].bitcast(f32), sub).then_inc(f_lo, 1)
                prep_lo(dve, U_MLP + 3, it, 4)
                if last:
                    return
                for s in range(2):
                    if s:
                        prep_lo(dve, U_MLP + 4, it, 4)
                    for t in range(NT):
                        n = FIRST["mlp"] + 8 + 8 * s + t
                        h = slice(s * 512, s * 512 + 512)
                        wait_full(dve, n, it, 24)
                        if s == 0 and t == 0:
                            dve.wait_ge(acc_zero, 1)
                        V.tensor_tensor(acc[:, t, h], banks[n % 8][:, :], acc[:, t, h], add).then_inc(bank_free[n % 8], 1)

            mlp(0, True, False)
            with dve.Fori(1, 7) as it:
                mlp(it, False, False)
            mlp(7, False, True)

            def scale(t):
                mark(V.tensor_tensor(yx[:, t % 2, :], acc[:, t, :], tok[:, 0:D], mul))

            def finish(t):
                xt = tok[:, (1 + t % 3) * D:(2 + t % 3) * D]
                dve.wait_ge(sq_o, NT + t + 1)
                rstd(sumsq[:, 26 + t:27 + t])
                dve.wait_ge(x1_back[t % 3], 16 * (t // 3 + 1))
                V.scalar_tensor_tensor(out=xt, in0=yx[:, t % 2, :], scalar=stat[:, 1:2], in1=xt, op0=mul, op1=add).then_inc(out_made, 1)

            dve.wait_ge(last_gain, 16)
            n_last = FIRST["mlp"] + 24 * 7 + 8
            for i, (t, s) in enumerate(LAST_DOWN):
                n, h = n_last + i, slice(s * 512, s * 512 + 512)
                wait_full(dve, n)
                V.tensor_tensor(acc[:, t, h], banks[n % 8][:, :], acc[:, t, h], add).then_inc(bank_free[n % 8], 1)
                if s == 0 and t >= 2:
                    finish(t - 1)
                if s == 1:
                    wait_taken(dve, n)
                    wait_taken(dve, n_last + LAST_DOWN.index((t, 0)))
                    dve.sem_inc(acc_done, 1)
                    scale(t)
                    if t == 1:
                        finish(0)
            finish(NT - 1)

        @block.tensor
        def _(pe):
            T = nc.tensor

            def product(dst, lhs, rhs, kt, start=True, stop=True, ready=None):
                for k in range(kt):
                    if ready:
                        ready(k)
                    for i, (p, q) in enumerate(((0, 0), (0, 1), (1, 0))):
                        ins = T.matmul(dst, lhs(k)[p], rhs(k)[q], start=start and k == 0 and i == 0,
                                       stop=stop and k == kt - 1 and i == 2)
                return ins

            def unit(u, it=0, per=0):
                pe.wait_ge(w_lo, u + 1 + it * per)

            def norm_event(idx, e):
                return FIRST["front"] + (2 * idx + e if idx < 2 else 6 + 6 * ((idx - 2) // 2) + 2 * ((idx - 2) % 2) + e)

            def transposes(n, srcs, dsts=None):
                wait_free(pe, n)
                for i, src in enumerate(srcs):
                    ins = T.transpose(banks[n % 8][:, i * P:i * P + P] if dsts is None else dsts[i], src, ident[:, :])
                ins.then_inc(bank_full[n % 8], 1)

            def norm_transposes(idx):
                pe.wait_ge(h_made, idx + 1)
                for e in range(2):
                    transposes(norm_event(idx, e), [hst[:, idx % 2, (4 * e + i) * P:(4 * e + i + 1) * P] for i in range(4)])

            hT = lambda sl: (lambda k: (hThi[:, k, sl], hTlo[:, k, sl]))
            half = lambda h: slice(h * 512, h * 512 + 512)

            pe.wait_ge(consts, 6)
            norm_transposes(0)
            norm_transposes(1)
            for idx in range(2):
                for e in range(2):
                    wait_taken(pe, norm_event(idx, e))
            for s in range(4):
                n0 = FIRST["front"] + 4 + 6 * s
                unit(s)
                hi, lo = wviews(s, KT)
                for i in range(2):
                    n = n0 + i
                    c = slice(i * P, i * P + P)
                    wait_free(pe, n)
                    if s < 2:
                        ins = product(banks[n % 8][:, 0:256], lambda k: (hi[:, k, c], lo[:, k, c]),
                                      lambda k: (mThi[:, k, :], mTlo[:, k, :]), KT)
                    else:
                        ins = product(banks[n % 8][:, 0:256], lambda k: (mThi[:, k, c], mTlo[:, k, c]),
                                      lambda k: (hi[:, k, :], lo[:, k, :]), KT)
                    ins.then_inc(bank_full[n % 8], 1)
                norm_transposes(2 + 2 * s)
                norm_transposes(3 + 2 * s)

            def project(u, n0):
                unit(u)
                w = [v.rearrange("p k (i c) -> p k i c", i=2) for v in wviews(u, KT)]
                for j in range(4):
                    n = n0 + j
                    wait_free(pe, n)
                    product(banks[n % 8][:, :], lambda k: (w[0][:, k, j // 2], w[1][:, k, j // 2]), hT(half(j % 2)), KT)\
                        .then_inc(bank_full[n % 8], 1)

            pe.wait_ge(s5_dt, 1)
            n = FIRST["spar"]
            wait_free(pe, n)
            for k in range(3):
                ins = T.transpose(banks[n % 8][:, 16 * k:16 * k + 16], sload[:, k, :], ident[0:NPAIR, 0:NPAIR])
            ins.then_inc(bank_full[n % 8], 1)
            for idx in range(2, 10):
                for e in range(2):
                    wait_taken(pe, norm_event(idx, e))
            for s in range(2):
                project(U_QX + s, FIRST["qx"] + 4 * s)
            tokq = tok[:, :].rearrange("p (i t) -> p i t", i=4)
            for n in range(FIRST["qx"], FIRST["qx"] + 8):
                wait_taken(pe, n)
            for e in range(16):
                n = FIRST["xsc"] + e
                wait_free(pe, n)
                for hh in range(2):
                    h = 2 * (e % 2) + hh
                    ins = T.matmul(banks[n % 8][:, hh * 256:hh * 256 + 256], tokq[:, h, (e // 2) * P:(e // 2 + 1) * P],
                                   kmT[:, h, :], start=True, stop=True)
                ins.then_inc(bank_full[n % 8], 1)
            for s in range(2):
                project(U_Q + s, FIRST["q"] + 4 * s)
            project(U_KV, FIRST["kv"])
            pe.wait_ge(x_prob, 16)

            def x_transposes(q):
                h, hf = q // 2, q % 2
                for m in range(2):
                    c = (h % 2) * 256 + m * P
                    transposes(FIRST["xpv"] + pv_event(q, m), [prob[:, 2 * (4 * hf + t) + h // 2, c:c + P] for t in range(4)])

            x_transposes(0)
            for q in range(8):
                if q < 7:
                    x_transposes(q + 1)
                n = FIRST["xpv"] + pv_event(q, 2)
                for m in range(2):
                    wait_taken(pe, FIRST["xpv"] + pv_event(q, m))
                wait_free(pe, n)
                h = q // 2
                for m in range(2):
                    ins = T.matmul(banks[n % 8][:, :], vm[:, m, h * P:h * P + P], pT[:, q % 2, m, :], start=m == 0, stop=m == 1)
                ins.then_inc(bank_full[n % 8], 1)
            for e in range(10):
                n = FIRST["rope"] + e
                src = qwin[:, e // 4, (e // 2) % 2, 8 * (e % 2):8 * (e % 2) + 8, :] if e < 8 else kT[:, half(e % 2)]
                wait_taken(pe, FIRST["q"] + e)
                wait_free(pe, n)
                T.matmul(banks[n % 8][:, :], rotm[:, :], src, start=True, stop=True).then_inc(bank_full[n % 8], 1)
            for n in (FIRST["kv"] + 2, FIRST["kv"] + 3):
                wait_taken(pe, n)
            for e in range(4):
                starts = [max(0, 64 * (4 * e + i - 1)) for i in range(4)]
                transposes(FIRST["vwin"] + e, [vT[:, s0:s0 + P] for s0 in starts])
            gates = lambda i: project(U_GATE[i], FIRST[f"g{i}"])
            gates(0)
            pe.wait_ge(rope_done, 10)
            for e in range(16):
                n = FIRST["ssc"] + e
                j = e % 2
                rows = slice(64 * j, 64 * j + 64)
                wait_free(pe, n)
                for sl in range(4):
                    ch, pair = 2 * (e // 2) + sl // 2, sl % 2
                    k0, nk = (0, 64) if ch == 0 else (64 * (ch - 1), P)
                    ins = T.matmul(banks[n % 8][:, sl * P:sl * P + nk], qflat[rows, pair, ch, :],
                                   kT[rows, k0:k0 + nk], start=True, stop=True)
                ins.then_inc(bank_full[n % 8], 1)
            hs = [h[:, :, :].rearrange("p k (c i) -> p k i c", i=STEP) for h in (hThi, hTlo)]
            for s in range(2):
                u = U_U + s
                unit(u)
                hi, lo = wviews(u, KT)
                for jj in range(4):
                    n = FIRST["u"] + 4 * s + jj
                    wait_free(pe, n)
                    for ii in range(2):
                        i = 2 * jj + ii
                        ins = product(banks[n % 8][:, ii * 256:ii * 256 + 256], lambda k: (hs[0][:, k, i, :], hs[1][:, k, i, :]),
                                      lambda k: (hi[:, k, :], lo[:, k, :]), KT)
                    ins.then_inc(bank_full[n % 8], 1)
            gates(1)
            pe.wait_ge(s_prob, 16)
            for e in range(4):
                wait_taken(pe, FIRST["vwin"] + e)

            def s_transposes(q):
                for nn in range(2):
                    n = FIRST["spv"] + pv_event(q, nn)
                    nk = 64 if q == 0 and nn == 0 else P
                    transposes(n, [prob[:, 2 * q + ja // 2, (2 * nn + ja % 2) * P:(2 * nn + ja % 2) * P + nk] for ja in range(4)],
                               [banks[n % 8][0:nk, ja * P:ja * P + P] for ja in range(4)])

            s_transposes(0)
            for q in range(8):
                if q < 7:
                    s_transposes(q + 1)
                n = FIRST["spv"] + pv_event(q, 2)
                for nn in range(2):
                    wait_taken(pe, FIRST["spv"] + pv_event(q, nn))
                wait_free(pe, n)
                for nn in range(2):
                    nk = 64 if q == 0 and nn == 0 else P
                    for j in range(2):
                        ins = T.matmul(banks[n % 8][64 * j:64 * j + 64, nn * 256:nn * 256 + 256],
                                       vwin[0:nk, 2 * q + nn, 64 * j:64 * j + 64], pT[0:nk, q % 2, nn, j * 256:j * 256 + 256],
                                       start=True, stop=True)
                ins.then_inc(bank_full[n % 8], 1)
            gates(2)
            pe.wait_ge(s5_in, 112)
            for ri in range(2):
                transposes(FIRST["spc"] + ri, [craw[:, ri, r, :, :].rearrange("p d x -> p (d x)") for r in range(4)])
            for n in range(FIRST["u"], FIRST["u"] + 8):
                wait_taken(pe, n)
            for r in range(4):
                n0 = FIRST[f"s5a{r}"]
                for e in range(2):
                    transposes(n0 + e, [uc[:, 8 * r + g, :, :].rearrange("p i c -> p (i c)") for g in range(4 * e, 4 * e + 4)])
                pe.wait_ge(s5_x, r + 1)
                for ri in range(2):
                    transposes(n0 + 2 + ri, [Xp[:, ri, q, 0:P] for q in range(RP)])
                for e in range(4):
                    wait_taken(pe, n0 + e)
                for e in range(2):
                    n = n0 + 4 + e
                    wait_free(pe, n)
                    for q in range(2):
                        for ri in range(2):
                            for g in range(2):
                                ins = T.matmul(banks[n % 8][64 * g:64 * g + 64, (2 * q + ri) * P:(2 * q + ri) * P + P],
                                               wT[:, ri, 2 * e + q, 64 * g:64 * g + 64], uT[:, 2 * (2 * e + q) + g, :],
                                               start=True, stop=True)
                    ins.then_inc(bank_full[n % 8], 1)
                gates(3 + 2 * r)
                pe.wait_ge(s5_ca, r + 1)
                pe.wait_ge(s5_near, 6 * (r + 1))
                cas = [ca[:, ri, :, :].rearrange("p a (g x) -> p a g x", g=2) for ri in range(2)]
                for e in range(2):
                    n = FIRST[f"s5m{r}"] + e
                    wait_free(pe, n)
                    for q in range(2):
                        pr = 2 * e + q
                        dst = banks[n % 8][:, q * 256:q * 256 + 256].rearrange("p (g x) -> p g x", g=2)
                        for kind, to, src in ((0, slice(SG, 8 * SG), slice(0, 7 * SG)), (1, slice(0, SG), slice(0, SG))):
                            for ri in range(2):
                                ins = T.matmul(dst[:, :, to], near[:, kind, ri, pr, :], cas[ri][:, pr, :, src],
                                               start=ri == 0, stop=ri == 1)
                    ins.then_inc(bank_full[n % 8], 1)
                gates(4 + 2 * r)
                for e in range(2):
                    wait_taken(pe, FIRST[f"s5m{r}"] + e)
                pe.wait_ge(s5_xs, r + 1)
                for e in range(2):
                    n = FIRST[f"s5y{r}"] + e
                    wait_free(pe, n)
                    for q in range(2):
                        pr = 2 * e + q
                        for ri in range(2):
                            T.matmul(banks[n % 8][:, q * 256:q * 256 + 256].rearrange("p (g x) -> p g x", g=2),
                                     xs[:, ri, pr, :], cas[ri][:, pr, :, SG:9 * SG],
                                     start=ri == 0, stop=False, skip_group_check=True)
                        for g in range(2):
                            ins = T.matmul(banks[n % 8][:, q * 256 + g * P:q * 256 + g * P + P], uT[:, 2 * pr + g, :], Mt[:, 2 * pr + g, :],
                                           start=False, stop=g == 1, skip_group_check=True)
                    ins.then_inc(bank_full[n % 8], 1)
            gates(11)
            for e in range(8):
                pe.wait_ge(gelu_done, e // 2 + 1)
                transposes(FIRST["yg"] + e, [gl[e // 2][:, 4 * (e % 2) + i, :] for i in range(4)])
            yT = lambda sl: (lambda k: (yhi[:, k, sl], ylo[:, k, sl]))
            mT = lambda sl: (lambda k: (hThi[:, 4 + k, sl], hTlo[:, 4 + k, sl]))

            def branch(stage, first, rhs, pieces):
                for s in range(2):
                    unit(first + s)
                    hi, lo = wviews(first + s, BT)
                    for j in range(8):
                        n = FIRST[stage] + 8 * s + j
                        c = slice((j // 2) * P, (j // 2) * P + P)
                        wait_free(pe, n)
                        if s == 0 and j == 0:
                            pe.wait_ge(y_lo, pieces)
                        product(banks[n % 8][:, :], lambda k: (hi[:, k, c], lo[:, k, c]), rhs(half(j % 2)), BT).then_inc(bank_full[n % 8], 1)

            branch("mergeA", U_MERGE_A, yT, 8)
            for e in range(8):
                wait_taken(pe, FIRST["yg"] + e)
            for s in range(2):
                u = U_GLU + s
                unit(u)
                hi, lo = wviews(u, BT)
                for j in range(4):
                    for ag in range(2):
                        n = FIRST["glu"] + 8 * s + 2 * j + ag
                        c = slice(ag * 256 + (j // 2) * P, ag * 256 + (j // 2) * P + P)
                        wait_free(pe, n)
                        product(banks[n % 8][:, :], lambda k: (hi[:, k, c], lo[:, k, c]), hT(half(j % 2)), BT).then_inc(bank_full[n % 8], 1)
            branch("mergeM", U_MERGE_M, mT, 16)
            branch("mergeS", U_MERGE_S, yT, 24)
            ring = [w[:, :, :].rearrange("p s (k c) -> p k s c", k=KT) for w in (whi, wlo)]
            kept = [y[:, :, :].rearrange("p (s a) (b c) -> p (a b) s c", s=2, c=256) for y in (yhi, ylo)]
            for e, s, number in ((0, 1, 0), (0, 0, 1), (1, 0, 2), (1, 1, 3)):
                unit(U_OUT + number)
                w = kept if e else ring
                for t in range(2):
                    n = out_event("w", t, e)
                    if number % 2 == 0:
                        wait_free(pe, n)
                    ready = (lambda k: pe.wait_ge(m_lo, k + 1)) if number == 0 and t == 0 else None
                    ins = product(banks[n % 8][:, s * 256:s * 256 + 256], hT(slice(t * P, t * P + P)),
                                  lambda k: (w[0][:, k, s, :], w[1][:, k, s, :]), KT, ready=ready)
                    if number % 2:
                        ins.then_inc(bank_full[n % 8], 1)

            def w_out(t, e):
                n = out_event("w", t, e)
                w = kept if e else ring
                wait_free(pe, n)
                product(banks[n % 8][:, :].rearrange("p (s c) -> p s c", s=2), hT(slice(t * P, t * P + P)),
                        lambda k: (w[0][:, k, :, :], w[1][:, k, :, :]), KT).then_inc(bank_full[n % 8], 1)

            def h2_transposes(t):
                pe.wait_ge(h2_made, t + 1)
                for e in range(2):
                    c = (2 + t % 2) * D + 4 * e * P
                    transposes(out_event("h", t, e), [tok[:, c + i * P:c + i * P + P] for i in range(4)])

            for step in OUT_ORDER[:-3]:
                t = int(step[1])
                if step[0] == "h":
                    h2_transposes(t)
                    continue
                for e in range(2 if t > 1 else 0):
                    w_out(t, e)

            for t in range(4):
                for e in range(2):
                    wait_taken(pe, out_event("h", t, e))

            def mlp(it, first, last):
                for s in range(2):
                    u = U_MLP + s
                    unit(u, it, 4)
                    hi, lo = wviews(u, KT)
                    for j in range(4):
                        n = FIRST["mlp"] + 4 * s + j
                        c = slice((j % 2) * P, (j % 2) * P + P)
                        if first and s == 0 and j == 2:
                            for t in range(5, NT):
                                h2_transposes(t)
                            for t in range(4, NT):
                                for e in range(2):
                                    wait_taken(pe, out_event("h", t, e))
                        wait_free(pe, n, it, 24)
                        product(banks[n % 8][:, :], lambda k: (hi[:, k, c], lo[:, k, c]), hT(half(j // 2)), KT).then_inc(bank_full[n % 8], 1)
                down = [(t, s) for s in range(2) for t in range(NT)] if not last else LAST_DOWN
                for i, (t, s) in enumerate(down):
                    n = FIRST["mlp"] + 8 + i
                    if (t, s) in ((0, 0), (0, 1)):
                        unit(U_MLP + 2 + s, it, 4)
                    hi, lo = wviews(U_MLP + 2 + s, BT)
                    wait_free(pe, n, it, 24)
                    if s == 0 and t in (0, 4):
                        pe.wait_ge(f_lo, it * 8 + (6 if t == 0 else 8))
                    product(banks[n % 8][:, :], yT(slice(t * P, t * P + P)), lambda k: (hi[:, k, :], lo[:, k, :]), BT)\
                        .then_inc(bank_full[n % 8], 1)

            mlp(0, True, False)
            with pe.Fori(1, 7) as it:
                mlp(it, False, False)
            mlp(7, False, True)


_INS = ["x", "mem", "positions", "g_mix_pre", "g_mix_post", "g_mem", "g_mlp_pre", "g_mlp_post", "sinks", "w_in", "w_mem_kv",
        "ssm_A_re", "ssm_A_im", "ssm_log_dt", "ssm_B_re", "ssm_B_im", "ssm_C_re", "ssm_C_im", "ssm_D", "w_glu",
        "w_branch_attn", "w_branch_ssm", "w_branch_mem", "w_out", "w_up", "w_down"]


def kernel(**inputs):
    import numpy as _np
    import concourse.bacc as _bacc
    from concourse import mybir as _mybir
    from concourse.bass_utils import run_bass_kernel_spmd as _run

    nc = _bacc.Bacc("TRN2", target_bir_lowering=False, num_devices=1)
    arrays, args = {}, {}
    for name in _INS:
        arrays[name] = _np.ascontiguousarray(inputs[name])
    freq = (10000.0 ** (-_np.arange(HD // 2, dtype=_np.float64) / (HD // 2))).astype(_np.float32)
    arrays["inv_freq"] = _np.tile(freq, P // (HD // 2)).reshape(P, 1)
    feed = {}
    for name, arr in arrays.items():
        feed[f"in_{name}_dram"] = arr
        args[name] = nc.dram_tensor(f"in_{name}_dram", arr.shape, _mybir.dt.from_np(arr.dtype), kind="ExternalInput").ap()
    out = nc.dram_tensor("out_0_dram", (1, L, D), _mybir.dt.float32, kind="ExternalOutput").ap()
    hybrid_layer(nc, args, out)
    r = _run(nc, [feed], core_ids=[0])
    return r.results[0]["out_0_dram"]
```
